# Optimizing a Trainium2 kernel written in Bass

```python
import jax, jax.numpy as jnp
from jax import lax
import numpy as np

D_MODEL = 2048
BATCH = 1
SEQ = 256
DEPTH = 1

RMS_EPS = 1e-6
ROPE_THETA = 10000.0
MIX_WIDTH = D_MODEL
HG_WIDTH = MIX_WIDTH // 2
HG_DK = 128
HG_DV = 128
HG_HEADS = HG_WIDTH // HG_DV
HG_CHUNK = 64
NSA_WIDTH = MIX_WIDTH - HG_WIDTH
NSA_DH = 64
NSA_HEADS = NSA_WIDTH // NSA_DH
NSA_KV = 2
NSA_REP = NSA_HEADS // NSA_KV
CMP_LEN = 32
CMP_STRIDE = 16
CMP_HIDDEN = 256
SEL_LEN = 64
SEL_TOP = 16
WINDOW = 512
Q_BLOCK = 128
MEM_LEN = 256
X_HEADS = 4
X_DH = 128
D_FF = ((8 * D_MODEL // 3) + 255) // 256 * 256
IN_SIZES = (HG_HEADS * HG_DK, HG_HEADS * HG_DK, HG_WIDTH, HG_WIDTH,
            NSA_WIDTH,
            NSA_KV * NSA_DH, NSA_KV * NSA_DH,
            NSA_KV * NSA_DH, NSA_KV * NSA_DH,
            NSA_KV * NSA_DH, NSA_KV * NSA_DH,
            NSA_HEADS * 3)
D_IN = sum(IN_SIZES)

kernel_name = "hybrid_hgrn2_nsa_macaron_layer"

def rmsnorm(x, w):
    xf = x.astype(jnp.float32)
    y = xf * lax.rsqrt(jnp.mean(xf * xf, axis=-1, keepdims=True) + RMS_EPS)
    return (y * w.astype(jnp.float32)).astype(x.dtype)

def swiglu(h, w_gate, w_up, w_down):
    return (jax.nn.silu(h @ w_gate) * (h @ w_up)) @ w_down

def rope(t, positions):
    half = t.shape[-1] // 2
    inv = ROPE_THETA ** (-jnp.arange(half, dtype=jnp.float32) / half)
    ang = positions.astype(jnp.float32)[..., None] * inv
    cos, sin = jnp.cos(ang)[:, :, None, :], jnp.sin(ang)[:, :, None, :]
    tf = t.astype(jnp.float32)
    t1, t2 = tf[..., :half], tf[..., half:]
    return jnp.concatenate([t1 * cos - t2 * sin, t2 * cos + t1 * sin], axis=-1).astype(t.dtype)

def masked_softmax(s, mask):
    s = jnp.where(mask, s.astype(jnp.float32), -jnp.inf)
    m = jnp.max(s, axis=-1, keepdims=True)
    m = jnp.where(jnp.isfinite(m), m, 0.0)
    e = jnp.where(mask, jnp.exp(s - m), 0.0)
    return e / jnp.maximum(jnp.sum(e, axis=-1, keepdims=True), 1e-30)

def hgrn2_mix(q, f_logit, i, g, lb, norm_w):
    B, S = q.shape[:2]
    nc = S // HG_CHUNK
    lb = lb.reshape(HG_HEADS, HG_DK)
    f = lb + (1.0 - lb) * jax.nn.sigmoid(f_logit.astype(jnp.float32))
    logf = jnp.log(f)
    k = 1.0 - f

    def chunks(t, d):
        return t.astype(jnp.float32).reshape(B, nc, HG_CHUNK, HG_HEADS, d).transpose(1, 0, 3, 2, 4)

    causal = jnp.tril(jnp.ones((HG_CHUNK, HG_CHUNK), dtype=bool))[:, :, None]

    def step(state, inp):
        qc, kc, lfc, vc = inp
        b = jnp.cumsum(lfc, axis=2)
        o_inter = jnp.einsum('bhck,bhkv->bhcv', qc * jnp.exp(b), state)
        diff = b[:, :, :, None, :] - b[:, :, None, :, :]
        decay = jnp.exp(jnp.where(causal, diff, -jnp.inf))
        att = jnp.einsum('bhtk,bhsk,bhtsk->bhts', qc, kc, decay)
        o_intra = jnp.einsum('bhts,bhsv->bhtv', att, vc)
        b_last = b[:, :, -1:, :]
        new_state = jnp.exp(b_last[:, :, 0, :])[..., None] * state + \
            jnp.einsum('bhsk,bhsv->bhkv', kc * jnp.exp(b_last - b), vc)
        return new_state, o_inter + o_intra

    state0 = jnp.zeros((B, HG_HEADS, HG_DK, HG_DV), jnp.float32)
    _, o = lax.scan(step, state0, (chunks(q, HG_DK), chunks(k, HG_DK), chunks(logf, HG_DK), chunks(i, HG_DV)))
    o = o.transpose(1, 0, 3, 2, 4).reshape(B, S, HG_HEADS, HG_DV)
    o = o * lax.rsqrt(jnp.mean(o * o, axis=-1, keepdims=True) + RMS_EPS)
    o = o.reshape(B, S, HG_WIDTH) * norm_w.astype(jnp.float32) * jax.nn.silu(g.astype(jnp.float32))
    return o.astype(q.dtype)

def nsa_mix(q, kc_tok, vc_tok, ks, vs, kw, vw, gate_logits, pe, ck_w1, ck_w2, cv_w1, cv_w2):
    B, S = q.shape[:2]
    G, R, dh = NSA_KV, NSA_REP, NSA_DH
    scale = dh ** -0.5
    n_cmp = (S - CMP_LEN) // CMP_STRIDE + 1
    n_sel = S // SEL_LEN
    n_top = min(SEL_TOP, n_sel)
    n_qb = S // Q_BLOCK

    cidx = jnp.arange(n_cmp)[:, None] * CMP_STRIDE + jnp.arange(CMP_LEN)[None, :]

    def compress(tok, w1, w2):
        blocks = tok[:, cidx] + pe[None, None, :, None, :]
        blocks = blocks.transpose(0, 1, 3, 2, 4).reshape(B, n_cmp, G, CMP_LEN * dh)
        return (jax.nn.silu(blocks @ w1) @ w2).transpose(0, 2, 1, 3)

    kc = compress(kc_tok, ck_w1, ck_w2)
    vc = compress(vc_tok, cv_w1, cv_w2)
    c_start = jnp.arange(n_cmp) * CMP_STRIDE
    cmp_end = c_start + CMP_LEN - 1
    s_start = jnp.arange(n_sel) * SEL_LEN
    overlap = jnp.clip(jnp.minimum(c_start[:, None] + CMP_LEN, s_start[None, :] + SEL_LEN)
                       - jnp.maximum(c_start[:, None], s_start[None, :]), 0, None).astype(jnp.float32) / CMP_LEN

    to_bg = lambda t: t.transpose(0, 2, 1, 3)
    ksb = to_bg(ks).reshape(B, G, n_sel, SEL_LEN, dh)
    vsb = to_bg(vs).reshape(B, G, n_sel, SEL_LEN, dh)
    kw_pad = jnp.pad(to_bg(kw), ((0, 0), (0, 0), (WINDOW, 0), (0, 0)))
    vw_pad = jnp.pad(to_bg(vw), ((0, 0), (0, 0), (WINDOW, 0), (0, 0)))
    qg = q.reshape(B, S, G, R, dh).transpose(0, 2, 3, 1, 4)
    bidx = jnp.arange(B)[:, None, None, None]
    gidx = jnp.arange(G)[None, :, None, None]
    blk_ids = jnp.arange(n_sel)

    def block(qb_i):
        q0 = qb_i * Q_BLOCK
        qb = lax.dynamic_slice_in_dim(qg, q0, Q_BLOCK, axis=3)
        tpos = q0 + jnp.arange(Q_BLOCK)
        s_c = jnp.einsum('bgrqd,bgnd->bgrqn', qb, kc) * scale
        p_c = masked_softmax(s_c, cmp_end[None, :] <= tpos[:, None])
        o_c = jnp.einsum('bgrqn,bgnd->bgrqd', p_c.astype(vc.dtype), vc)
        imp = jnp.einsum('bgrqn,nj->bgqj', p_c, overlap)
        cur = tpos // SEL_LEN
        forced = (blk_ids[None, :] == 0) | (blk_ids[None, :] == cur[:, None]) | (blk_ids[None, :] == cur[:, None] - 1)
        future = blk_ids[None, :] > cur[:, None]
        score = jnp.where(forced, jnp.inf, jnp.where(future, -jnp.inf, imp))
        _, sel = lax.top_k(score, n_top)
        k_sel = ksb[bidx, gidx, sel]
        v_sel = vsb[bidx, gidx, sel].reshape(B, G, Q_BLOCK, n_top * SEL_LEN, dh)
        tok = sel[..., None] * SEL_LEN + jnp.arange(SEL_LEN)
        mask_s = (tok <= tpos[None, None, :, None, None]).reshape(B, G, 1, Q_BLOCK, n_top * SEL_LEN)
        s_s = jnp.einsum('bgrqd,bgqntd->bgrqnt', qb, k_sel).reshape(B, G, R, Q_BLOCK, n_top * SEL_LEN) * scale
        p_s = masked_softmax(s_s, mask_s)
        o_s = jnp.einsum('bgrqm,bgqmd->bgrqd', p_s.astype(v_sel.dtype), v_sel)
        kwb = lax.dynamic_slice_in_dim(kw_pad, q0, Q_BLOCK + WINDOW, axis=2)
        vwb = lax.dynamic_slice_in_dim(vw_pad, q0, Q_BLOCK + WINDOW, axis=2)
        kpos = q0 - WINDOW + jnp.arange(Q_BLOCK + WINDOW)
        dpos = tpos[:, None] - kpos[None, :]
        mask_w = (dpos >= 0) & (dpos < WINDOW) & (kpos[None, :] >= 0)
        s_w = jnp.einsum('bgrqd,bgkd->bgrqk', qb, kwb) * scale
        p_w = masked_softmax(s_w, mask_w)
        o_w = jnp.einsum('bgrqk,bgkd->bgrqd', p_w.astype(vwb.dtype), vwb)
        return jnp.stack([o_c, o_s, o_w], axis=0)

    outs = lax.map(block, jnp.arange(n_qb))
    outs = outs.transpose(1, 2, 0, 5, 3, 4, 6).reshape(3, B, S, NSA_HEADS, dh)
    gates = jax.nn.sigmoid(gate_logits.reshape(B, S, NSA_HEADS, 3)).transpose(3, 0, 1, 2)[..., None]
    o = jnp.sum(gates.astype(outs.dtype) * outs, axis=0)
    return o.reshape(B, S, NSA_WIDTH)

def mem_cross_attn(h, m, wq, wk, wv, wo):
    B, S, _ = h.shape
    M = m.shape[1]
    q = (h @ wq).reshape(B, S, X_HEADS, X_DH)
    k = (m @ wk).reshape(B, M, X_HEADS, X_DH)
    v = (m @ wv).reshape(B, M, X_HEADS, X_DH)
    s = jnp.einsum('bshd,bmhd->bhsm', q, k) * (X_DH ** -0.5)
    p = jax.nn.softmax(s.astype(jnp.float32), axis=-1).astype(v.dtype)
    o = jnp.einsum('bhsm,bmhd->bshd', p, v).reshape(B, S, X_HEADS * X_DH)
    return o @ wo

def setup_inputs(seed: int = 0) -> dict:
    key = jax.random.key(seed)
    k = jax.random.split(key, 30)
    f32 = jnp.float32
    L = DEPTH

    def w(kk, shape, fan_in):
        return jax.random.normal(kk, shape, f32) * fan_in ** -0.5

    def gain(kk, shape):
        return 1.0 + 0.01 * jax.random.normal(kk, shape, f32)

    x = jax.random.normal(k[0], (BATCH, SEQ, D_MODEL), f32)
    mem = jax.random.normal(k[1], (BATCH, MEM_LEN, D_MODEL), f32)
    positions = (jax.random.randint(k[2], (BATCH, 1), 0, 1024, dtype=jnp.int32)
                 + jnp.arange(SEQ, dtype=jnp.int32)[None, :]).astype(jnp.int32)
    return {
        'x': x, 'mem': mem, 'positions': positions,
        'ffn1_norm': gain(k[3], (L, D_MODEL)),
        'ffn1_w_gate': w(k[4], (L, D_MODEL, D_FF), D_MODEL),
        'ffn1_w_up': w(k[5], (L, D_MODEL, D_FF), D_MODEL),
        'ffn1_w_down': w(k[6], (L, D_FF, D_MODEL), D_FF),
        'mix_norm': gain(k[7], (L, D_MODEL)),
        'w_in': w(k[8], (L, D_MODEL, D_IN), D_MODEL),
        'hgrn_lb_logits': 0.5 * jax.random.normal(k[9], (L + 1, HG_HEADS * HG_DK), f32),
        'hgrn_out_norm': gain(k[10], (L, HG_WIDTH)),
        'nsa_cmp_pe': 0.1 * jax.random.normal(k[11], (L, CMP_LEN, NSA_DH), f32),
        'nsa_cmp_k_w1': w(k[12], (L, CMP_LEN * NSA_DH, CMP_HIDDEN), CMP_LEN * NSA_DH),
        'nsa_cmp_k_w2': w(k[13], (L, CMP_HIDDEN, NSA_DH), CMP_HIDDEN),
        'nsa_cmp_v_w1': w(k[14], (L, CMP_LEN * NSA_DH, CMP_HIDDEN), CMP_LEN * NSA_DH),
        'nsa_cmp_v_w2': w(k[15], (L, CMP_HIDDEN, NSA_DH), CMP_HIDDEN),
        'w_out': w(k[16], (L, MIX_WIDTH, D_MODEL), MIX_WIDTH),
        'xattn_norm': gain(k[17], (L, D_MODEL)),
        'mem_norm': gain(k[18], (L, D_MODEL)),
        'xattn_wq': w(k[19], (L, D_MODEL, X_HEADS * X_DH), D_MODEL),
        'xattn_wk': w(k[20], (L, D_MODEL, X_HEADS * X_DH), D_MODEL),
        'xattn_wv': w(k[21], (L, D_MODEL, X_HEADS * X_DH), D_MODEL),
        'xattn_wo': w(k[22], (L, X_HEADS * X_DH, D_MODEL), X_HEADS * X_DH),
        'ffn2_norm': gain(k[23], (L, D_MODEL)),
        'ffn2_w_gate': w(k[24], (L, D_MODEL, D_FF), D_MODEL),
        'ffn2_w_up': w(k[25], (L, D_MODEL, D_FF), D_MODEL),
        'ffn2_w_down': w(k[26], (L, D_FF, D_MODEL), D_FF),
        'final_norm': gain(k[27], (D_MODEL,)),
    }

def reference(x, mem, positions, ffn1_norm, ffn1_w_gate, ffn1_w_up, ffn1_w_down, mix_norm, w_in,
              hgrn_lb_logits, hgrn_out_norm, nsa_cmp_pe, nsa_cmp_k_w1, nsa_cmp_k_w2, nsa_cmp_v_w1,
              nsa_cmp_v_w2, w_out, xattn_norm, mem_norm, xattn_wq, xattn_wk, xattn_wv, xattn_wo,
              ffn2_norm, ffn2_w_gate, ffn2_w_up, ffn2_w_down, final_norm):
    B, S, _ = x.shape
    lb_all = jnp.cumsum(jax.nn.softmax(hgrn_lb_logits.astype(jnp.float32), axis=0), axis=0)
    split_at = [int(v) for v in np.cumsum(IN_SIZES)[:-1]]
    kv_heads = lambda t: t.reshape(B, S, NSA_KV, NSA_DH)
    for l in range(DEPTH):
        x = x + 0.5 * swiglu(rmsnorm(x, ffn1_norm[l]), ffn1_w_gate[l], ffn1_w_up[l], ffn1_w_down[l])
        h = rmsnorm(x, mix_norm[l])
        hq, hf, hi, hg, nq, nkc, nvc, nks, nvs, nkw, nvw, ngate = jnp.split(h @ w_in[l], split_at, axis=-1)
        o_hg = hgrn2_mix(hq.reshape(B, S, HG_HEADS, HG_DK), hf.reshape(B, S, HG_HEADS, HG_DK),
                         hi.reshape(B, S, HG_HEADS, HG_DV), hg, lb_all[l], hgrn_out_norm[l])
        o_nsa = nsa_mix(rope(nq.reshape(B, S, NSA_HEADS, NSA_DH), positions),
                        rope(kv_heads(nkc), positions), kv_heads(nvc),
                        rope(kv_heads(nks), positions), kv_heads(nvs),
                        rope(kv_heads(nkw), positions), kv_heads(nvw), ngate,
                        nsa_cmp_pe[l], nsa_cmp_k_w1[l], nsa_cmp_k_w2[l], nsa_cmp_v_w1[l], nsa_cmp_v_w2[l])
        x = x + jnp.concatenate([o_hg, o_nsa], axis=-1) @ w_out[l]
        x = x + mem_cross_attn(rmsnorm(x, xattn_norm[l]), rmsnorm(mem, mem_norm[l]),
                               xattn_wq[l], xattn_wk[l], xattn_wv[l], xattn_wo[l])
        x = x + 0.5 * swiglu(rmsnorm(x, ffn2_norm[l]), ffn2_w_gate[l], ffn2_w_up[l], ffn2_w_down[l])
    return rmsnorm(x, final_norm)


_drawn_inputs = setup_inputs


def setup_inputs(seed=0):
    import zlib

    import numpy as np

    out = dict(_drawn_inputs(seed))
    spreads = {}
    factors = {'ffn1_norm': 8.0,
     'mix_norm': 6.747,
     'hgrn_out_norm': 25.608,
     'nsa_cmp_pe': 10.021,
     'xattn_norm': 23.284,
     'mem_norm': 24.875,
     'ffn2_norm': 61.256,
     'final_norm': 31.838}
    for name, (base, spread) in spreads.items():
        noise = np.random.default_rng([zlib.crc32(name.encode()), seed]).standard_normal(out[name].shape)
        drawn = base * np.exp(spread * noise) if base else spread * noise
        out[name] = __import__('jax').numpy.asarray(drawn.astype(out[name].dtype))
    for name, factor in factors.items():
        out[name] = (out[name] * factor).astype(out[name].dtype)
    return out
```

```python
from contextlib import ExitStack

import concourse.bass as bass
from concourse import mybir

P = 128
F32 = mybir.dt.float32
F32R = mybir.dt.float32r
I32 = mybir.dt.int32
U8 = mybir.dt.uint8
ALU = mybir.AluOpType
ACT = mybir.ActivationFunctionType
AX_X = mybir.AxisListType.X

D = 2048
SEQ = 256
NT = SEQ // P
MEM = 256
EPS = 1e-6
D_FF = 5632
HG_HEADS, HG_D = 8, 128
HG_W = HG_HEADS * HG_D
NSA_HEADS, NSA_KV, DH = 16, 2, 64
REP = NSA_HEADS // NSA_KV
CMP_LEN, CMP_STRIDE, CMP_HIDDEN = 32, 16, 256
N_CMP = (SEQ - CMP_LEN) // CMP_STRIDE + 1
CPAD = 16
X_HEADS, X_DH = 4, 128
D_IN = 4 * HG_W + NSA_HEADS * DH + 6 * NSA_KV * DH + NSA_HEADS * 3
C_NSA = 4 * HG_W
C_KV = NSA_HEADS * DH
C_GATE = C_KV + 6 * NSA_KV * DH
W_NSA = C_GATE + NSA_HEADS * 3
NEG = -1e30
TWO_PI = 6.283185307179586
PI_A = 6.28125
PI_B = 0.00193500518798828125
PI_C = TWO_PI - PI_A - PI_B
ROUND = 12582912.0

NW = 512
KT_U = 2
SLOTS = 4
KD = D // P
KF = D_FF // P
U_G = KD // KT_U
U_D = KF // KT_U
FF_CHUNKS = D_FF // NW
D_CHUNKS = D // NW
IN_GROUPS = ([(C_NSA + C_KV, NW), (C_NSA + C_KV + NW, D_IN - C_NSA - C_KV - NW),
              (C_NSA, NW), (C_NSA + NW, NW)]
             + [(c, NW) for c in (1024, 1536, 0, 512, 2048, 2560, 3072, 3584)])
U_MEMK = 0
U_MEMV = U_MEMK + U_G
U_GU1 = U_MEMV + U_G
U_DN1 = U_GU1 + 2 * U_G * FF_CHUNKS
U_IN = U_DN1 + U_D * D_CHUNKS
U_CMP = U_IN + U_G * len(IN_GROUPS)
U_OUT = U_CMP + U_G
U_XQ = U_OUT + U_G * D_CHUNKS
U_XO = U_XQ + U_G
U_XOG = X_HEADS // KT_U
U_GU2 = U_XO + U_XOG * D_CHUNKS
U_DN2 = U_GU2 + 2 * U_G * FF_CHUNKS
U_END = U_DN2 + U_D * D_CHUNKS

B_MEM = 0
B_KX = B_MEM + 4
B_X = B_KX + 1
B_H1 = B_X + 4
B_MIXN = B_H1 + FF_CHUNKS
B_MIX = B_MIXN + 4
B_XAN = B_MIX + 4
B_F2N = B_XAN + 4
B_H2 = B_F2N + 4

V_F1, V_MIX, V_XA, V_MEM, V_F2, V_LB, V_PE, V_HG = 0, 16, 32, 48, 64, 80, 96, 112
V_ROWS = 120
N_MEM, N_F1, N_MIX, N_XA, N_F2, N_FIN = range(6)
LEVELS = [1, 2, 4, 8, 16, 32, 64]


def layer_program(nc, a, c, out):
    with ExitStack() as ctx:
        def sem(name):
            return ctx.enter_context(nc.semaphore(name))

        arena = ctx.enter_context(nc.sbuf_tensor("arena", [P, 206 * 1024], U8))
        base = (nc.sbuf_base - 206 * 1024 + 63) // 64 * 64
        at = [base]

        def put(name, shape, dt, size=4):
            n = size
            for s in shape[1:]:
                n *= s
            t = nc.alloc_sbuf_tensor_at(name, shape, dt, offset=at[0])
            at[0] += (n + 31) // 32 * 32
            return t

        x = put("x", [P, NT, D], F32)
        xT_hi = put("xT_hi", [P, KD, SEQ], F32R)
        xT_lo = put("xT_lo", [P, KD, SEQ], F32R)
        w_raw = put("w_raw", [P, SLOTS, KT_U, NW], F32)
        w_hi = put("w_hi", [P, SLOTS, KT_U, NW], F32R)
        w_lo = put("w_lo", [P, SLOTS, KT_U, NW], F32R)
        sg = put("silu_gate", [P, NT, NW], F32)
        hb = put("ff_hidden", [P, NT, NW], F32)
        keep = at[0]
        kxT = put("kxT", [P, X_HEADS, MEM], F32)
        vx = put("vx", [P, MEM // P, X_HEADS * X_DH], F32)
        fnorm = nc.alloc_sbuf_tensor_at("final_norm_rows", [P, D], F32, offset=keep)
        ident = put("ident", [P, P], F32)
        causal = put("causal", [P, SEQ], F32)
        cmp_add = put("cmp_add", [P, NT, N_CMP], F32)
        cmp_mul = put("cmp_mul", [P, NT, N_CMP], F32)
        diag_blk = put("diag_blk", [P, REP], F32)
        inv_f = put("inv_f", [P, DH // 2], F32)
        pos_i = put("pos_i", [P, NT], I32)
        pos_f = put("pos_f", [P, NT], F32)
        vec = put("vec", [P, V_ROWS], F32)
        sin_t = put("sin_t", [P, NT, DH // 2], F32)
        cos_t = put("cos_t", [P, NT, DH // 2], F32)
        ss = put("ss", [P, 6, NT, 4], F32)
        var = put("var", [P, 6, NT], F32)
        std = put("std", [P, 6, NT], F32)
        rstd = put("rstd", [P, 6, NT], F32)
        lb_w = put("lb_w", [P, 5, HG_HEADS], F32)
        w2 = put("w2", [P, 2, 2, DH], F32)
        ff = at[0]
        ffT_hi = put("ffT_hi", [P, KF, SEQ], F32R)
        ffT_lo = put("ffT_lo", [P, KF, SEQ], F32R)
        ff_end = at[0]
        assert ff_end <= base + 206 * 1024, ff_end - base

        def place(name, shape, off, dt=F32):
            n = 1 if dt == U8 else 4
            for s in shape[1:]:
                n *= s
            assert ff + off + n <= ff_end, name
            return nc.alloc_sbuf_tensor_at(name, shape, dt, offset=ff + off)

        mem_x = place("mem_x", [P, NT, D], 0)
        vec_rows = place("vec_rows", [P, P], 16384)
        ang = place("ang", [P, 4, NT, DH // 2], 16896)
        z_qf = place("z_qf", [P, NT, 2 * HG_W], 0)
        z_ig = place("z_ig", [P, NT, 2 * HG_W], 16384)
        z_n = place("z_n", [P, NT, W_NSA], 32768)
        o1 = 32768 + 4 * NT * W_NSA
        qT = place("qT", [P, REP, SEQ], o1)
        kT = place("kT", [P, 2, NSA_KV, SEQ], o1 + 8192)
        rtmp = place("rtmp", [P, 4, NSA_HEADS * DH // 2], o1 + 12288)
        blk = place("blk", [P, KD, 66], o1 + 12288)
        blk_hi = place("blk_hi", [P, KD, 66], o1 + 16640, F32R)
        blk_lo = place("blk_lo", [P, KD, 66], o1 + 20992, F32R)
        o2 = o1 + 25344
        hid = place("hid", [P, CMP_HIDDEN], o2)
        hidT = place("hidT", [P, 2, 64], o2 + 1024)
        hid_rep = place("hid_rep", [P, 2, NSA_KV, REP * N_CMP], o2 + 1536)
        kcT = place("kcT", [P, 32], o2 + 3456)
        v_blk = place("v_blk", [P, NSA_KV, REP * DH], o2 + 3584)
        gate = place("gate", [P, NT, NSA_HEADS, 3], o2 + 7680)
        mx = place("mx", [P, NT, NSA_HEADS, 2], o2 + 8064)
        sm = place("sm", [P, NT, NSA_HEADS, 2], o2 + 8320)
        rc = place("rc", [P, NT, NSA_HEADS, 2], o2 + 8576)
        cstat = place("cstat", [P, NT, 2, NSA_HEADS], o2 + 8832)
        pc = place("pc", [P, NT, NSA_HEADS * N_CMP], o2 + 9088)
        pcT = place("pcT", [P, NT, NSA_KV, P], o2 + 11008)
        prob = [place("prob0", [P, 2, 512], o1 + 12288), place("prob1", [P, 2, 512], o1 + 16640)]
        probT = place("probT", [P, 2, 512], o1 + 20992)
        fT = place("fT", [P, HG_HEADS, SEQ], o1)
        qfT = place("qfT", [P, HG_HEADS, SEQ], o1 + 8192)
        kgT = place("kgT", [P, HG_HEADS, SEQ], o1 + 16384)
        tots = {1: fT}
        o3 = o1 + 24576
        for m in LEVELS[1:]:
            tots[m] = place(f"tot{m}", [P, HG_HEADS, SEQ // m], o3)
            o3 += 4 * HG_HEADS * SEQ // m
        hst = place("hst", [P, 4, NT, HG_HEADS], o3)
        att = place("att", [P, HG_HEADS, NT, P], 0)
        att_x = place("att_x", [P, HG_HEADS, P], 8192)
        lvl_f32 = place("lvl_f32", [P, len(LEVELS), P // 2], 86016)
        lvl_mask = place("lvl_mask", [P, len(LEVELS), P // 2], 88064, U8)
        qx = place("qx", [P, NT, X_HEADS * X_DH], 16384)
        qxT = place("qxT", [P, X_HEADS, SEQ], 20480)
        px = place("px", [P, X_HEADS, NT, MEM], 67584)
        pxT = place("pxT", [P, X_HEADS, MEM // P, SEQ], 24576)
        xst = place("xst", [P, 3, X_HEADS, NT], 67584 + 8192)
        MIX_HI, MIX_LO, OX = 0, 6, 40
        MEM_T = 28

        psum = ctx.enter_context(nc.psum_tensor("psum", [P, 8, 512], F32))
        pair = [psum[:, 0:2, :], psum[:, 2:4, :]]
        turn = [psum[:, 4:6, :].rearrange("p b (k t) -> p (b k) t", t=SEQ),
                psum[:, 6:8, :].rearrange("p b (k t) -> p (b k) t", t=SEQ)]

        w_loaded = [sem(f"w_loaded{i}") for i in range(SLOTS)]
        w_hi_ready = sem("w_hi_ready")
        w_lo_ready = sem("w_lo_ready")
        unit_done = sem("unit_done")
        turned = sem("turned")
        turn_hi = sem("turn_hi")
        turn_lo = sem("turn_lo")
        const_loaded = sem("const_loaded")
        mask_loaded = sem("mask_loaded")
        mem_loaded = [sem(f"mem_loaded{i}") for i in range(4)]
        x_loaded = [sem(f"x_loaded{i}") for i in range(4)]
        vec_turned = sem("vec_turned")
        vec_ready = sem("vec_ready")
        sq_done = sem("sq_done")
        var_ready = sem("var_ready")
        std_ready = sem("std_ready")
        rstd_ready = sem("rstd_ready")
        trig_args = sem("trig_args")
        trig_ready = sem("trig_ready")
        lb_exp = sem("lb_exp")
        kv_taken = sem("kv_taken")
        gate_ready = sem("gate_ready")
        h_ready = sem("h_ready")
        x_ready = sem("x_ready")
        z_ready = sem("z_ready")
        dve_step = sem("dve_step")
        act_step = sem("act_step")
        roped = sem("roped")
        q_turned = sem("q_turned")
        q_taken = sem("q_taken")
        k_turned = sem("k_turned")
        k_taken = sem("k_taken")
        tok_turned = sem("tok_turned")
        blk_ready = sem("blk_ready")
        blk_hi_ready = sem("blk_hi_ready")
        blk_lo_ready = sem("blk_lo_ready")
        hid_ready = sem("hid_ready")
        hid_turned = sem("hid_turned")
        hidT_ready = sem("hidT_ready")
        kvc_done = sem("kvc_done")
        kvc_ready = sem("kvc_ready")
        sc_done = sem("sc_done")
        sc_ready = sem("sc_ready")
        ec_ready = sem("ec_ready")
        pc_ready = sem("pc_ready")
        pc_turned = sem("pc_turned")
        pcT_ready = sem("pcT_ready")
        gates_ready = sem("gates_ready")
        s_done = sem("s_done")
        s_taken = sem("s_taken")
        e_ready = sem("e_ready")
        p_ready = sem("p_ready")
        p_turned = sem("p_turned")
        pT_ready = sem("pT_ready")
        pv_done = sem("pv_done")
        o_taken = sem("o_taken")
        f_turned = sem("f_turned")
        f_sig = sem("f_sig")
        hq_turned = sem("hq_turned")
        hq_taken = sem("hq_taken")
        kf_ready = sem("kf_ready")
        dg_done = sem("dg_done")
        dg_taken = sem("dg_taken")
        qk_ready = sem("qk_ready")
        lv_done = sem("lv_done")
        lv_taken = sem("lv_taken")
        cross_done = sem("cross_done")
        cross_taken = sem("cross_taken")
        ho_done = sem("ho_done")
        ho_sq = sem("ho_sq")
        ho_var = sem("ho_var")
        ho_std = sem("ho_std")
        g_silu = sem("g_silu")
        mix_ready = sem("mix_ready")
        qx_ready = sem("qx_ready")
        qx_turned = sem("qx_turned")
        qx_taken = sem("qx_taken")
        xs_done = sem("xs_done")
        xm_ready = sem("xm_ready")
        xe_ready = sem("xe_ready")
        xp_ready = sem("xp_ready")
        xp_turned = sem("xp_turned")
        xpT_ready = sem("xpT_ready")
        xo_done = sem("xo_done")
        xo_hi = sem("xo_hi")
        xo_lo = sem("xo_lo")
        fn_loaded = sem("fn_loaded")
        out_ready = sem("out_ready")
        stored = sem("stored")

        block = ctx.enter_context(nc.Block())

        def cols(w, j, c0, width):
            return w[KT_U * P * j:KT_U * P * (j + 1), c0:c0 + width].rearrange("(k p) n -> p k n", p=P)

        def dyn_cols(w, j, chunk):
            return w[KT_U * P * j:KT_U * P * (j + 1), bass.ts(chunk, NW)].rearrange("(k p) n -> p k n", p=P)

        @block.sync
        def _(sp):
            def load(u, slot, src, first=False):
                if not first:
                    sp.wait_ge(w_lo_ready, u - (SLOTS - 1))
                sp.dma_start(w_raw[:, slot, :, 0:src.shape[2]], src).then_inc(w_loaded[slot], 16)

            for g, w in enumerate((a["wk"], a["wv"])):
                for j in range(U_G):
                    u = U_MEMK + U_G * g + j
                    load(u, u % SLOTS, cols(w, j, 0, NW), first=u < SLOTS)

            def gate_up(u0, wg, wu):
                with sp.Fori(0, FF_CHUNKS) as ch:
                    for k, w in enumerate((wg, wu)):
                        for j in range(U_G):
                            kk = U_G * k + j
                            load(u0 + 2 * U_G * ch + kk, (u0 + kk) % SLOTS, dyn_cols(w, j, ch))

            def down(u0, w):
                for n in range(D_CHUNKS):
                    for j in range(U_D):
                        u = u0 + U_D * n + j
                        load(u, u % SLOTS, cols(w, j, n * NW, NW))

            gate_up(U_GU1, a["g1"], a["u1"])
            down(U_DN1, a["d1"])
            for n, (c0, width) in enumerate(IN_GROUPS):
                for j in range(U_G):
                    u = U_IN + U_G * n + j
                    load(u, u % SLOTS, cols(a["w_in"], j, c0, width))
            sp.wait_ge(z_ready, 1)
            sp.dma_start(lvl_f32[:], c["lvl_mask"]).then_inc(mask_loaded, 16)
            for j in range(U_G):
                load(U_CMP + j, (U_CMP + j) % SLOTS, cols(a["cw1"], j, 0, NW))
            for n in range(D_CHUNKS):
                for j in range(U_G):
                    u = U_OUT + U_G * n + j
                    load(u, u % SLOTS, cols(a["w_out"], j, n * NW, NW))
            for j in range(U_G):
                load(U_XQ + j, (U_XQ + j) % SLOTS, cols(a["wq"], j, 0, NW))
            for n in range(D_CHUNKS):
                for j in range(U_XOG):
                    u = U_XO + U_XOG * n + j
                    load(u, u % SLOTS, cols(a["wo"], j, n * NW, NW))
            gate_up(U_GU2, a["g2"], a["u2"])
            sp.wait_ge(xo_lo, 1)
            sp.dma_start(fnorm[:], a["fn"].rearrange("(o n) -> o n", o=1).broadcast_to([P, D]))\
              .then_inc(fn_loaded, 16)
            down(U_DN2, a["d2"])
            for t in range(NT):
                sp.wait_ge(out_ready, t + 1)
                sp.dma_start(out[t * P:(t + 1) * P, :], x[:, t, :]).then_inc(stored, 16)
            sp.wait_ge(stored, 16 * NT)

        @block.scalar
        def _(act):
            chain = [0]

            def link(ins):
                chain[0] += 1
                ins.then_inc(act_step, 1)
                act.wait_ge(act_step, chain[0])

            def split(u, slot, turn_no, first=False):
                act.wait_ge(w_loaded[slot], 16 * turn_no)
                if not first:
                    act.wait_ge(unit_done, u - (SLOTS - 1))
                nc.scalar.activation(w_hi[:, slot], w_raw[:, slot], ACT.Copy).then_inc(w_hi_ready, 1)

            def step(u):
                if u + SLOTS < U_END:
                    split(u + SLOTS, u % SLOTS, u // SLOTS + 2)

            def take(b, pos, dst, kt, scale=None, junk=None):
                act.wait_ge(turned, b + 1)
                if scale is None:
                    nc.scalar.activation(dst[:, kt:kt + 4, :] if isinstance(kt, int) else dst[:, bass.ts(kt[0], 4), :],
                                         turn[pos], ACT.Copy).then_inc(turn_hi, 1)
                    return
                for j in range(4):
                    last = nc.scalar.activation(dst[:, kt + j, :], turn[pos][:, j, :], ACT.Copy,
                                                scale=vec[:, scale + j:scale + j + 1])
                last.then_inc(turn_hi, 1)

            def squares(src, norm, n):
                for t in range(NT):
                    last = nc.scalar.activation(sg[:, t, :], src[:, t, n * NW:(n + 1) * NW], ACT.Square,
                                                accum_out=ss[:, norm, t, n:n + 1])
                last.then_inc(sq_done, 1)
                sq[0] += 1
                act.wait_ge(sq_done, sq[0])

            sq = [0]

            def root(norm):
                act.wait_ge(var_ready, norm + 1)
                nc.scalar.activation(std[:, norm, :], var[:, norm, :], ACT.Sqrt).then_inc(std_ready, 1)

            act.dma_start(ident[:], c["ident"]).then_inc(const_loaded, 16)
            for r0, name, n in ((V_F1, "n1", 16), (V_MIX, "nm", 16), (V_XA, "nx", 16), (V_MEM, "nmem", 16),
                                (V_F2, "n2", 16), (V_LB, "lb", 16), (V_HG, "nhg", 8)):
                act.dma_start(vec_rows[r0:r0 + n, :], a[name].rearrange("(r p) -> r p", p=P))\
                   .then_inc(const_loaded, 16)
            act.dma_start(vec_rows[V_PE:V_PE + 16, :], a["pe"].rearrange("(r p) -> r p", p=P))\
               .then_inc(const_loaded, 16)
            for n in range(4):
                act.dma_start(mem_x[:, :, n * NW:(n + 1) * NW],
                              a["mem"][:, n * NW:(n + 1) * NW].rearrange("(t p) n -> p t n", p=P))\
                   .then_inc(mem_loaded[n], 16)
            act.dma_start(pos_i[:], a["pos"].rearrange("(t p) -> p t", p=P), allow_slow_non_contiguous=True).then_inc(const_loaded, 16)
            for dst, name in ((inv_f, "inv_f"), (causal, "causal"), (cmp_add, "cmp_add"), (cmp_mul, "cmp_mul"),
                              (diag_blk, "diag_blk")):
                act.dma_start(dst[:], c[name]).then_inc(const_loaded, 16)
            for i, name in enumerate(("kw2", "vw2")):
                act.dma_start(w2[:, i], a[name].rearrange("(k p) n -> p k n", p=P)).then_inc(const_loaded, 16)
            for n in range(4):
                act.dma_start(x[:, :, n * NW:(n + 1) * NW],
                              a["x"][:, n * NW:(n + 1) * NW].rearrange("(t p) n -> p t n", p=P))\
                   .then_inc(x_loaded[n], 16)

            for n in range(4):
                act.wait_ge(mem_loaded[n], 16)
                squares(mem_x, N_MEM, n)
                if n == 0:
                    act.wait_ge(vec_ready, 1)
                take(B_MEM + n, n % 2, ffT_hi, MEM_T + 4 * n, V_MEM + 4 * n)
                split(n, n, 1, first=True)
            root(N_MEM)
            act.wait_ge(lb_exp, 1)
            nc.scalar.activation(lb_w[:, 2:4, :], lb_w[:, 0:2, :], ACT.Exp).then_inc(lb_exp, 1)
            for j in range(U_G):
                step(U_MEMK + j)
            for j in range(U_G):
                step(U_MEMV + j)
                if j == 2:
                    act.wait_ge(turned, B_KX + 1)
                    nc.scalar.activation(kxT[:, 0:2, :], turn[0][:, 0:2, :], ACT.Copy).then_inc(turn_hi, 1)
                if j >= 3 and j < 7:
                    n = j - 3
                    act.wait_ge(x_loaded[n], 16)
                    squares(x, N_F1, n)
                    take(B_X + n, (n + 1) % 2, xT_hi, 4 * n, V_F1 + 4 * n)
            root(N_F1)
            act.wait_ge(trig_args, 1)
            nc.scalar.activation(sin_t[:], ang[:, 1], ACT.Sin)
            nc.scalar.activation(cos_t[:], ang[:, 2], ACT.Sin).then_inc(trig_ready, 1)

            def ffn_up(u0, norm, b_h, b_x3, s_x3, base_c):
                def body(ch, first):
                    for k in range(2 * U_G):
                        u = u0 + 2 * U_G * ch + k
                        split(u + SLOTS, (u0 + k) % SLOTS, (u0 + k) // SLOTS + 2 + (2 * U_G // SLOTS) * ch)
                        if k == 4:
                            if not first:
                                take(b_h - 1 + ch, 0, ffT_hi, (ch - 1,))
                            elif b_x3 is not None:
                                squares_take3()
                        if k == U_G - 1:
                            act.wait_ge(unit_done, u + 1)
                            if first:
                                if base_c:
                                    act.wait_ge(h_ready, base_c)
                            else:
                                act.wait_ge(h_ready, base_c + ch)
                            for t in range(NT):
                                last = nc.scalar.activation(sg[:, t, :], pair[0][:, t, :], ACT.Silu,
                                                            scale=rstd[:, norm, t:t + 1])
                            last.then_inc(gate_ready, 1)

                def squares_take3():
                    take(b_x3, 0, xT_hi, 12, s_x3 + 12)
                    root(norm)
                    act.wait_ge(rstd_ready, norm + 1)

                if b_x3 is None:
                    act.wait_ge(rstd_ready, norm + 1)
                body(0, True)
                with act.Fori(1, FF_CHUNKS) as ch:
                    body(ch, False)

            def ffn_down(u0, norm, b_h, b_x, s_x, xr):
                for n in range(D_CHUNKS):
                    for k in range(U_D):
                        step(u0 + U_D * n + k)
                        if k == 4:
                            if n == 0:
                                take(b_h + FF_CHUNKS - 1, 0, ffT_hi, KF - 4)
                            elif b_x is not None:
                                take(b_x + n - 1, 0, xT_hi, 4 * (n - 1), s_x + 4 * (n - 1))
                    act.wait_ge(x_ready, xr + n + 1)
                    squares(x, norm, n)

            ffn_up(U_GU1, N_F1, B_H1, None, None, 0)
            ffn_down(U_DN1, N_MIX, B_H1, B_MIXN, V_MIX, 0)

            for n in range(len(IN_GROUPS)):
                for j in range(U_G):
                    step(U_IN + U_G * n + j)
                    if n == 0 and j == 4:
                        take(B_MIXN + 3, 0, xT_hi, 12, V_MIX + 12)
                        root(N_MIX)

            act.wait_ge(z_ready, len(IN_GROUPS))
            for t in range(NT):
                last = nc.scalar.activation(gate[:, t], z_n[:, t, C_GATE:].rearrange("p (h b) -> p h b", b=3),
                                            ACT.Sigmoid)
            last.then_inc(gates_ready, 1)
            for b in range(2):
                act.wait_ge(q_turned, b + 1)
                nc.scalar.activation(qT[:, 4 * b:4 * b + 4, :], turn[b], ACT.Copy).then_inc(q_taken, 1)
            act.wait_ge(k_turned, 1)
            nc.scalar.activation(kT[:].rearrange("p b g s -> p (b g) s"), turn[0], ACT.Copy).then_inc(k_taken, 1)
            act.wait_ge(blk_ready, 1)
            nc.scalar.activation(blk_hi[:], blk[:], ACT.Copy).then_inc(blk_hi_ready, 1)
            for j in range(U_G):
                step(U_CMP + j)
            act.wait_ge(unit_done, U_CMP + U_G)
            nc.scalar.activation(hid[0:32, :], psum[0:32, 0, 0:CMP_HIDDEN], ACT.Silu)
            nc.scalar.activation(hid[32:64, :], psum[32:64, 0, CMP_HIDDEN:2 * CMP_HIDDEN], ACT.Silu)\
              .then_inc(hid_ready, 1)
            for t in range(NT):
                act.wait_ge(sc_ready, t + 1)
                nc.scalar.activation(pc[:, t, :], pc[:, t, :], ACT.Exp, scale=DH ** -0.5).then_inc(ec_ready, 1)
            act.wait_ge(pc_turned, 1)
            nc.scalar.activation(pcT[0:REP * N_CMP], psum[0:REP * N_CMP, 6, :].rearrange("p (t g s) -> p t g s", t=NT, g=2),
                                 ACT.Copy).then_inc(pcT_ready, 1)

            def width(i):
                return P if i < 8 else 2 * P

            def exps(i):
                t, h0 = i // 8, 2 * (i % 8)
                act.wait_ge(s_taken, i + 1)
                for hh in range(2):
                    for b in range(2):
                        w = width(i)
                        r = prob[i % 2][:, hh, b * w:(b + 1) * w]
                        last = nc.scalar.activation(r, r, ACT.Exp, scale=DH ** -0.5,
                                                    bias=mx[:, t, h0 + hh, b:b + 1],
                                                    accum_out=sm[:, t, h0 + hh, b:b + 1])
                last.then_inc(e_ready, 1)

            def takeT(m):
                act.wait_ge(p_turned, m + 1)
                if m >= 2:
                    act.wait_ge(pv_done, m - 1)
                w = 2 * width(m // 2)
                nc.scalar.activation(probT[:, m % 2, 0:w], psum[:, 6, 0:w], ACT.Copy).then_inc(pT_ready, 1)

            for i in range(17):
                if i < 16:
                    exps(i)
                if i >= 1:
                    takeT(2 * i - 2)
                    takeT(2 * i - 1)

            for b in range(2):
                act.wait_ge(f_turned, b + 1)
                nc.scalar.activation(fT[:, 4 * b:4 * b + 4, :], turn[b], ACT.Sigmoid).then_inc(f_sig, 1)
            for b in range(2):
                act.wait_ge(hq_turned, b + 1)
                nc.scalar.activation(qfT[:, 4 * b:4 * b + 4, :], turn[b], ACT.Copy).then_inc(hq_taken, 1)
            for t in range(NT):
                last = nc.scalar.activation(z_ig[:, t, HG_W:], z_ig[:, t, HG_W:], ACT.Silu)
            last.then_inc(g_silu, 1)
            act.wait_ge(cross_done, 1)
            nc.scalar.activation(att_x[:].rearrange("p h s -> p (h s)"),
                                 psum[:, 4:6, :].rearrange("p b n -> p (b n)"), ACT.Copy).then_inc(cross_taken, 1)
            for t in range(NT):
                act.wait_ge(ho_done, t + 1)
                nc.scalar.activation(fT[:, 4 * t:4 * t + 4, :].rearrange("p h s -> p (h s)"),
                                     psum[:, 4 + 2 * t:6 + 2 * t, :].rearrange("p b n -> p (b n)"),
                                     ACT.Square).then_inc(ho_sq, 1)
            act.wait_ge(ho_var, 1)
            nc.scalar.activation(hst[:, 2], hst[:, 1], ACT.Sqrt).then_inc(ho_std, 1)
            for n in range(4):
                take(B_MIX + n, n % 2, ffT_hi, MIX_HI + 4 * n, V_HG + 4 * n if n < 2 else None)

            for n in range(D_CHUNKS):
                for j in range(U_G):
                    step(U_OUT + U_G * n + j)
                    if j == 4 and n:
                        take(B_XAN + n - 1, 0, xT_hi, 4 * (n - 1), V_XA + 4 * (n - 1))
                act.wait_ge(x_ready, 4 + n + 1)
                squares(x, N_XA, n)
            for j in range(U_G):
                step(U_XQ + j)
                if j == 4:
                    take(B_XAN + 3, 0, xT_hi, 12, V_XA + 12)
                    root(N_XA)
            act.wait_ge(qx_turned, 1)
            nc.scalar.activation(qxT[:], turn[0], ACT.Copy).then_inc(qx_taken, 1)
            for h in range(X_HEADS):
                act.wait_ge(xm_ready, h + 1)
                for t in range(NT):
                    last = nc.scalar.activation(px[:, h, t, :], psum[:, 4 + h, t * MEM:(t + 1) * MEM], ACT.Exp,
                                                scale=X_DH ** -0.5, bias=xst[:, 0, h, t:t + 1],
                                                accum_out=xst[:, 1, h, t:t + 1])
                last.then_inc(xe_ready, 1)
            for h in range(X_HEADS):
                act.wait_ge(xp_turned, h + 1)
                nc.scalar.activation(pxT[:, h].rearrange("p k s -> p (k s)"), psum[:, 4 + h, :], ACT.Copy)\
                  .then_inc(xpT_ready, 1)
            act.wait_ge(xo_done, 1)
            nc.scalar.activation(ffT_hi[:, OX:OX + 4, :], turn[0], ACT.Copy).then_inc(xo_hi, 1)
            for n in range(D_CHUNKS):
                for j in range(U_XOG):
                    step(U_XO + U_XOG * n + j)
                act.wait_ge(x_ready, 8 + n + 1)
                squares(x, N_F2, n)
                if n:
                    take(B_F2N + n - 1, 0, xT_hi, 4 * (n - 1), V_F2 + 4 * (n - 1))

            ffn_up(U_GU2, N_F2, B_H2, B_F2N + 3, V_F2, FF_CHUNKS)
            ffn_down(U_DN2, N_FIN, B_H2, None, None, 12)
            root(N_FIN)

        @block.vector
        def _(dve):
            chain = [0]

            def link(ins):
                chain[0] += 1
                ins.then_inc(dve_step, 1)
                dve.wait_ge(dve_step, chain[0])

            def split(u, slot):
                dve.wait_ge(w_hi_ready, u + 1)
                nc.vector.tensor_tensor(w_lo[:, slot], w_raw[:, slot], w_hi[:, slot].bitcast(F32), ALU.subtract)\
                  .then_inc(w_lo_ready, 1)

            def step(u):
                if u + SLOTS < U_END:
                    split(u + SLOTS, u % SLOTS)

            def take(b, pos, lo, klo, hi, khi, scale=None):
                dve.wait_ge(turn_hi, b + 1)
                if scale is None:
                    dyn = not isinstance(klo, int)
                    lo_v = lo[:, bass.ts(klo[0], 4), :] if dyn else lo[:, klo:klo + 4, :]
                    hi_v = hi[:, bass.ts(khi[0], 4), :] if dyn else hi[:, khi:khi + 4, :]
                    nc.vector.tensor_tensor(lo_v, turn[pos], hi_v.bitcast(F32), ALU.subtract).then_inc(turn_lo, 1)
                    return
                for j in range(4):
                    last = nc.vector.scalar_tensor_tensor(
                        out=lo[:, klo + j, :], in0=turn[pos][:, j, :], scalar=vec[:, scale + j:scale + j + 1],
                        in1=hi[:, khi + j, :].bitcast(F32), op0=ALU.mult, op1=ALU.subtract)
                last.then_inc(turn_lo, 1)

            def variance(norm, sq):
                dve.wait_ge(sq_done, sq)
                link(nc.vector.tensor_reduce(var[:, norm, :], ss[:, norm], AX_X, ALU.add))
                nc.vector.tensor_scalar(var[:, norm, :], var[:, norm, :], 1.0 / D, EPS, ALU.mult, ALU.add)\
                  .then_inc(var_ready, 1)

            def inverse(norm):
                dve.wait_ge(std_ready, norm + 1)
                nc.vector.reciprocal(rstd[:, norm, :], std[:, norm, :]).then_inc(rstd_ready, 1)
                dve.wait_ge(rstd_ready, norm + 1)

            dve.wait_ge(vec_turned, 1)
            nc.vector.tensor_copy(vec[:], psum[:, 7, 0:V_ROWS]).then_inc(vec_ready, 1)
            for n in range(4):
                take(B_MEM + n, n % 2, ffT_lo, MEM_T + 4 * n, ffT_hi, MEM_T + 4 * n, V_MEM + 4 * n)
                split(n, n)
            variance(N_MEM, 4)
            dve.wait_ge(vec_ready, 1)
            l0, l1 = vec[:, V_LB:V_LB + 8], vec[:, V_LB + 8:V_LB + 16]
            link(nc.vector.tensor_tensor(lb_w[:, 4, :], l0, l1, ALU.max))
            nc.vector.tensor_tensor(lb_w[:, 0, :], l0, lb_w[:, 4, :], ALU.subtract)
            nc.vector.tensor_tensor(lb_w[:, 1, :], l1, lb_w[:, 4, :], ALU.subtract).then_inc(lb_exp, 1)
            inverse(N_MEM)
            dve.wait_ge(lb_exp, 2)
            link(nc.vector.tensor_tensor(lb_w[:, 4, :], lb_w[:, 2, :], lb_w[:, 3, :], ALU.add))
            link(nc.vector.reciprocal(lb_w[:, 4, :], lb_w[:, 4, :]))
            link(nc.vector.tensor_tensor(lb_w[:, 0, :], lb_w[:, 2, :], lb_w[:, 4, :], ALU.mult))
            link(nc.vector.tensor_scalar(lb_w[:, 1, :], lb_w[:, 0, :], -1.0, 1.0, ALU.mult, ALU.add))
            dve.wait_ge(const_loaded, 16 * 17)
            link(nc.vector.tensor_copy(pos_f[:], pos_i[:]))
            for t in range(NT):
                last = nc.vector.tensor_scalar(ang[:, 0, t, :], inv_f[:], pos_f[:, t:t + 1], None, ALU.mult)
            link(last)
            a0, a1, a2, a3 = (ang[:, i] for i in range(4))
            link(nc.vector.tensor_scalar(a3, a0, 1.0 / TWO_PI, ROUND, ALU.mult, ALU.add))
            link(nc.vector.tensor_scalar(a3, a3, -ROUND, None, ALU.add))
            for part, (src, dst) in zip((PI_A, PI_B, PI_C), ((a0, a1), (a1, a2), (a2, a1))):
                link(nc.vector.scalar_tensor_tensor(out=dst, in0=a3, scalar=-part, in1=src,
                                                    op0=ALU.mult, op1=ALU.add))
            link(nc.vector.tensor_scalar(a1, a1, 3.14159, -3.14159, ALU.min, ALU.max))
            link(nc.vector.scalar_tensor_tensor(out=a2, in0=a1, scalar=-1.0, in1=a1, op0=ALU.mult, op1=ALU.min))
            nc.vector.tensor_scalar(a2, a2, TWO_PI / 4, None, ALU.add).then_inc(trig_args, 1)
            for j in range(U_G):
                step(U_MEMK + j)
            dve.wait_ge(unit_done, U_MEMK + U_G)
            for t in range(NT):
                last = nc.vector.tensor_scalar(hb[:, t, :], pair[0][:, t, :], rstd[:, N_MEM, t:t + 1], None, ALU.mult)
            last.then_inc(kv_taken, 1)
            for j in range(U_G):
                step(U_MEMV + j)
                if j == 2:
                    dve.wait_ge(turn_hi, B_KX + 1)
                    nc.vector.tensor_copy(kxT[:, 2:4, :], turn[0][:, 2:4, :]).then_inc(turn_lo, 1)
                if j >= 3 and j < 7:
                    n = j - 3
                    take(B_X + n, (n + 1) % 2, xT_lo, 4 * n, xT_hi, 4 * n, V_F1 + 4 * n)
            variance(N_F1, 8)
            dve.wait_ge(unit_done, U_MEMV + U_G)
            for t in range(NT):
                last = nc.vector.tensor_scalar(vx[:, t, :], pair[1][:, t, :], rstd[:, N_MEM, t:t + 1], None, ALU.mult)
            last.then_inc(kv_taken, 1)
            inverse(N_F1)

            def ffn_up(u0, norm, b_h, b_x3, s_x3, base_c, sq):
                def body(ch, first):
                    for k in range(2 * U_G):
                        u = u0 + 2 * U_G * ch + k
                        split(u + SLOTS, (u0 + k) % SLOTS)
                        if k == 4:
                            if not first:
                                take(b_h - 1 + ch, 0, ffT_lo, (ch - 1,), ffT_hi, (ch - 1,))
                            elif b_x3 is not None:
                                take(b_x3, 0, xT_lo, 12, xT_hi, 12, s_x3 + 12)
                                variance(norm, sq)
                                inverse(norm)
                    dve.wait_ge(unit_done, u + 1)
                    dve.wait_ge(gate_ready, base_c + 1 + ch)
                    dve.wait_ge(turned, b_h + ch)
                    for t in range(NT):
                        last = nc.vector.scalar_tensor_tensor(
                            out=hb[:, t, :], in0=pair[1][:, t, :], scalar=rstd[:, norm, t:t + 1],
                            in1=sg[:, t, :], op0=ALU.mult, op1=ALU.mult)
                    last.then_inc(h_ready, 1)

                body(0, True)
                with dve.Fori(1, FF_CHUNKS) as ch:
                    body(ch, False)

            def residual(src, n, factor):
                for t in range(NT):
                    xc = x[:, t, n * NW:(n + 1) * NW]
                    last = nc.vector.scalar_tensor_tensor(out=xc, in0=src[:, t, :], scalar=factor, in1=xc,
                                                          op0=ALU.mult, op1=ALU.add)
                last.then_inc(x_ready, 1)

            def ffn_down(u0, b_h, b_x, s_x):
                for n in range(D_CHUNKS):
                    for k in range(U_D):
                        step(u0 + U_D * n + k)
                        if k == 4:
                            if n == 0:
                                take(b_h + FF_CHUNKS - 1, 0, ffT_lo, KF - 4, ffT_hi, KF - 4)
                            elif b_x is not None:
                                take(b_x + n - 1, 0, xT_lo, 4 * (n - 1), xT_hi, 4 * (n - 1), s_x + 4 * (n - 1))
                    dve.wait_ge(unit_done, u0 + U_D * (n + 1))
                    residual(pair[n % 2], n, 0.5)

            ffn_up(U_GU1, N_F1, B_H1, None, None, 0, 8)
            ffn_down(U_DN1, B_H1, B_MIXN, V_MIX)

            for n, (c0, width) in enumerate(IN_GROUPS):
                for j in range(U_G):
                    step(U_IN + U_G * n + j)
                    if n == 0 and j == 4:
                        take(B_MIXN + 3, 0, xT_lo, 12, xT_hi, 12, V_MIX + 12)
                        variance(N_MIX, 12)
                        inverse(N_MIX)
                dve.wait_ge(unit_done, U_IN + U_G * (n + 1))
                dst, d0 = (z_n, c0 - C_NSA) if c0 >= C_NSA else (z_ig, c0 - 2048) if c0 >= 2048 else (z_qf, c0)
                for t in range(NT):
                    last = nc.vector.tensor_scalar(dst[:, t, d0:d0 + width], pair[n % 2][:, t, 0:width],
                                                   rstd[:, N_MIX, t:t + 1], None, ALU.mult)
                last.then_inc(z_ready, 1)
            dve.wait_ge(z_ready, len(IN_GROUPS))

            dve.wait_ge(trig_ready, 1)
            for t in range(NT):
                qv = z_n[:, t, 0:C_KV].rearrange("p (h x d) -> p h x d", x=2, d=DH // 2)
                kv = z_n[:, t, C_KV:C_GATE].rearrange("p (a b g x d) -> p a b g x d", a=3, b=2, g=2, x=2)
                for part in range(4):
                    v, n = (qv, NSA_HEADS) if part == 0 else (kv[:, part - 1, 0], NSA_KV)
                    t1, t2 = v[:, :, 0, :], v[:, :, 1, :]
                    tmp = [rtmp[:, i, 0:n * DH // 2].rearrange("p (h d) -> p h d", d=DH // 2) for i in range(4)]
                    cosb = cos_t[:, t, :].unsqueeze(1).broadcast_to([P, n, DH // 2])
                    sinb = sin_t[:, t, :].unsqueeze(1).broadcast_to([P, n, DH // 2])
                    nc.vector.tensor_tensor(tmp[0], t1, cosb, ALU.mult)
                    nc.vector.tensor_tensor(tmp[1], t2, sinb, ALU.mult)
                    nc.vector.tensor_tensor(tmp[2], t2, cosb, ALU.mult)
                    link(nc.vector.tensor_tensor(tmp[3], t1, sinb, ALU.mult))
                    nc.vector.tensor_tensor(t1, tmp[0], tmp[1], ALU.subtract)
                    link(nc.vector.tensor_tensor(t2, tmp[2], tmp[3], ALU.add))
            nc.vector.memset(blk[:], 0.0).then_inc(roped, 1)
            dve.wait_ge(roped, 1)
            dve.wait_ge(tok_turned, 1)
            pe_t = vec[:, V_PE:V_PE + 16]
            for xg in range(4):
                for e in range(2):
                    last = nc.vector.tensor_tensor(
                        blk[:, 8 * e:8 * e + 8, xg * CPAD:xg * CPAD + N_CMP],
                        psum[:, 6, xg * P + 8 * e:xg * P + 8 * e + 8 * N_CMP].rearrange("p (n b) -> p b n", b=8),
                        pe_t[:, 8 * e:8 * e + 8].unsqueeze(2).broadcast_to([P, 8, N_CMP]), ALU.add)
            last.then_inc(blk_ready, 1)
            dve.wait_ge(blk_hi_ready, 1)
            nc.vector.tensor_tensor(blk_lo[:], blk[:], blk_hi[:].bitcast(F32), ALU.subtract).then_inc(blk_lo_ready, 1)
            for j in range(U_G):
                step(U_CMP + j)
            dve.wait_ge(hid_turned, 1)
            hid_ps = psum[:, 4, 0:128].rearrange("p (k r) -> p k r", k=2)
            nc.vector.tensor_copy(hidT[:], hid_ps)
            for k in range(2):
                for g in range(NSA_KV):
                    last = nc.vector.tensor_copy(
                        hid_rep[:, k, g, :].rearrange("p (r n) -> p r n", n=N_CMP),
                        hid_ps[:, k, 32 + g * CPAD:32 + g * CPAD + N_CMP].unsqueeze(1).broadcast_to([P, REP, N_CMP]))
            last.then_inc(hidT_ready, 1)
            dve.wait_ge(kvc_done, 1)
            nc.vector.tensor_copy(kcT[:], psum[:, 5, 0:32])
            n_rows = REP * N_CMP
            for g in range(NSA_KV):
                last = nc.vector.tensor_tensor(
                    v_blk[0:n_rows, g, :].rearrange("p (r d) -> p r d", d=DH),
                    psum[0:n_rows, 5, 64 + g * DH:64 + (g + 1) * DH].unsqueeze(1).broadcast_to([n_rows, REP, DH]),
                    diag_blk[0:n_rows, :].unsqueeze(2).broadcast_to([n_rows, REP, DH]), ALU.mult)
            last.then_inc(kvc_ready, 1)
            dve.wait_ge(gates_ready, 1)
            for t in range(NT):
                p3 = pc[:, t, :].rearrange("p (h n) -> p h n", n=N_CMP)
                sh = [P, NSA_HEADS, N_CMP]
                cm, cs = cstat[:, t, 0, :], cstat[:, t, 1, :]
                dve.wait_ge(sc_done, NT)
                link(nc.vector.tensor_tensor(
                    pc[:, t, :].rearrange("p (j e n) -> p e j n", e=2, n=N_CMP),
                    psum[:, 6:8, t * REP * N_CMP:(t + 1) * REP * N_CMP].rearrange("p e (j n) -> p e j n", n=N_CMP),
                    cmp_add[:, t, :].unsqueeze(1).unsqueeze(1).broadcast_to([P, 2, REP, N_CMP]), ALU.add))
                link(nc.vector.tensor_reduce(cm, p3, AX_X, ALU.max))
                nc.vector.tensor_tensor(p3, p3, cm.unsqueeze(2).broadcast_to(sh), ALU.subtract).then_inc(sc_ready, 1)
            for t in range(NT):
                p3 = pc[:, t, :].rearrange("p (h n) -> p h n", n=N_CMP)
                cm, cs = cstat[:, t, 0, :], cstat[:, t, 1, :]
                dve.wait_ge(ec_ready, t + 1)
                link(nc.vector.tensor_tensor(p3, p3, cmp_mul[:, t, :].unsqueeze(1).broadcast_to(sh), ALU.mult))
                link(nc.vector.tensor_reduce(cs, p3, AX_X, ALU.add))
                link(nc.vector.tensor_scalar(cs, cs, 1e-30, None, ALU.max))
                link(nc.vector.reciprocal(cs, cs))
                link(nc.vector.tensor_tensor(cs, cs, gate[:, t, :, 0], ALU.mult))
                nc.vector.tensor_tensor(p3, p3, cs.unsqueeze(2).broadcast_to(sh), ALU.mult).then_inc(pc_ready, 1)

            def maxima(i):
                t, h0 = i // 8, 2 * (i % 8)
                w = P if t == 0 else 2 * P
                dve.wait_ge(s_done, i + 1)
                if i >= 2:
                    dve.wait_ge(p_turned, 2 * (i - 1))
                for hh in range(2):
                    for b in range(2):
                        last = nc.vector.tensor_tensor_reduce(
                            out=prob[i % 2][:, hh, b * w:(b + 1) * w], in0=psum[:, 4 + hh, b * w:(b + 1) * w],
                            in1=causal[:, SEQ - w:SEQ], scale=1.0, scalar=-3e38, op0=ALU.add, op1=ALU.max,
                            accum_out=mx[:, t, h0 + hh, b:b + 1])
                link(last)
                nc.vector.tensor_scalar(mx[:, t, h0:h0 + 2, :], mx[:, t, h0:h0 + 2, :], -DH ** -0.5, None, ALU.mult)\
                  .then_inc(s_taken, 1)

            def weigh(i):
                t, h0 = i // 8, 2 * (i % 8)
                w = P if t == 0 else 2 * P
                r = rc[:, t, h0:h0 + 2, :]
                dve.wait_ge(e_ready, i + 1)
                link(nc.vector.tensor_scalar(r, sm[:, t, h0:h0 + 2, :], 1e-30, None, ALU.max))
                link(nc.vector.reciprocal(r, r))
                link(nc.vector.tensor_tensor(r, r, gate[:, t, h0:h0 + 2, 1:3], ALU.mult))
                for hh in range(2):
                    for b in range(2):
                        p = prob[i % 2][:, hh, b * w:(b + 1) * w]
                        last = nc.vector.tensor_scalar(p, p, rc[:, t, h0 + hh, b:b + 1], None, ALU.mult)
                last.then_inc(p_ready, 1)

            def take_o(k):
                t, g = k // 2, k % 2
                dve.wait_ge(pv_done, REP * (k + 1))
                nc.vector.tensor_copy(z_n[:, t, g * 512:(g + 1) * 512], psum[:, 7, :]).then_inc(o_taken, 1)

            for i in range(17):
                if i < 16:
                    maxima(i)
                if i >= 1:
                    weigh(i - 1)
                if i >= 5 and i % 4 == 1:
                    take_o(i // 4 - 1)
            take_o(3)

            dve.wait_ge(f_sig, 2)
            for h in range(HG_HEADS):
                last = nc.vector.tensor_scalar(fT[:, h, :], fT[:, h, :], lb_w[:, 1, h:h + 1], lb_w[:, 0, h:h + 1],
                                               ALU.mult, ALU.add)
            link(last)
            nc.vector.tensor_scalar(kgT[:], fT[:], -1.0, 1.0, ALU.mult, ALU.add).then_inc(kf_ready, 1)
            for b in range(4):
                dve.wait_ge(dg_done, b + 1)
                nc.vector.tensor_tensor(att[:, 2 * b:2 * b + 2].rearrange("p h t s -> p (h t) s"),
                                        psum[:, 4 + b, :].rearrange("p (c s) -> p c s", s=P),
                                        ident[:].unsqueeze(1).broadcast_to([P, 4, P]), ALU.mult).then_inc(dg_taken, 1)
            nc.vector.tensor_tensor(qfT[:], qfT[:], fT[:], ALU.mult).then_inc(qk_ready, 1)
            dve.wait_ge(mask_loaded, 16)
            link(nc.vector.tensor_copy(lvl_mask[:], lvl_f32[:]))
            for l, m in enumerate(LEVELS):
                dve.wait_ge(qk_ready, l + 1)
                dve.wait_ge(lv_done, 2 * (l + 1))
                q4 = qfT[:].rearrange("p h (b x m) -> p (h b) x m", x=2, m=m)
                k4 = kgT[:].rearrange("p h (b x m) -> p (h b) x m", x=2, m=m)
                t4 = tots[m][:].rearrange("p h (b x) -> p (h b) x", x=2)
                nb = HG_HEADS * SEQ // (2 * m)
                if m < LEVELS[-1]:
                    nc.vector.tensor_tensor(tots[2 * m][:].rearrange("p h b -> p (h b)"), t4[:, :, 0], t4[:, :, 1], ALU.mult)
                nc.vector.tensor_tensor(q4[:, :, 1, :], q4[:, :, 1, :], t4[:, :, 0].unsqueeze(2).broadcast_to([P, nb, m]),
                                        ALU.mult)
                nc.vector.tensor_tensor(k4[:, :, 0, :], k4[:, :, 0, :], t4[:, :, 1].unsqueeze(2).broadcast_to([P, nb, m]),
                                        ALU.mult).then_inc(qk_ready, 1)
                if l:
                    dve.wait_ge(lv_taken, 2 * l)
                for half in range(2):
                    a5 = att[:, 4 * half:4 * half + 4].rearrange("p h t (b x m) -> p (h t) b x m", x=2, m=m)
                    m4 = lvl_mask[:, l, :].rearrange("p (b m) -> p b m", m=m).unsqueeze(1)
                    nc.vector.copy_predicated(
                        a5[:, :, :, 1, :], m4.broadcast_to([P, 8, P // (2 * m), m]),
                        psum[:, 4 + (2 * l + half) % 4, :].rearrange("p (c b m) -> p c b m", c=8, m=m))\
                      .then_inc(lv_taken, 1)
            for t in range(NT):
                dve.wait_ge(ho_sq, t + 1)
                last = nc.vector.tensor_reduce(hst[:, 0, t, :], fT[:, 4 * t:4 * t + 4, :].rearrange("p h (x d) -> p (h x) d", x=2),
                                               AX_X, ALU.add)
            link(last)
            nc.vector.tensor_scalar(hst[:, 1], hst[:, 0], 1.0 / HG_D, EPS, ALU.mult, ALU.add).then_inc(ho_var, 1)
            dve.wait_ge(ho_std, 1)
            link(nc.vector.reciprocal(hst[:, 3], hst[:, 2]))
            for t in range(NT):
                o3v = psum[:, 4 + 2 * t:6 + 2 * t, :].rearrange("p b (h d) -> p (b h) d", d=HG_D)
                last = nc.vector.tensor_tensor(z_ig[:, t, 0:HG_W].rearrange("p (h d) -> p h d", d=HG_D), o3v,
                                               hst[:, 3, t, :].unsqueeze(2).broadcast_to([P, HG_HEADS, HG_D]), ALU.mult)
            link(last)
            dve.wait_ge(g_silu, 1)
            nc.vector.tensor_tensor(z_ig[:, :, HG_W:], z_ig[:, :, HG_W:], z_ig[:, :, 0:HG_W], ALU.mult)\
              .then_inc(mix_ready, 1)
            for n in range(4):
                take(B_MIX + n, n % 2, ffT_lo, MIX_LO + 4 * n, ffT_hi, MIX_HI + 4 * n, V_HG + 4 * n if n < 2 else None)

            for n in range(D_CHUNKS):
                for j in range(U_G):
                    step(U_OUT + U_G * n + j)
                    if j == 4 and n:
                        take(B_XAN + n - 1, 0, xT_lo, 4 * (n - 1), xT_hi, 4 * (n - 1), V_XA + 4 * (n - 1))
                dve.wait_ge(unit_done, U_OUT + U_G * (n + 1))
                residual(pair[n % 2], n, 1.0)
            for j in range(U_G):
                step(U_XQ + j)
                if j == 4:
                    take(B_XAN + 3, 0, xT_lo, 12, xT_hi, 12, V_XA + 12)
                    variance(N_XA, 16)
                    inverse(N_XA)
            dve.wait_ge(unit_done, U_XQ + U_G)
            for t in range(NT):
                last = nc.vector.tensor_scalar(qx[:, t, :], pair[0][:, t, :], rstd[:, N_XA, t:t + 1], None, ALU.mult)
            last.then_inc(qx_ready, 1)
            for h in range(X_HEADS):
                dve.wait_ge(xs_done, h + 1)
                link(nc.vector.tensor_reduce(xst[:, 2, h, :], psum[:, 4 + h, :].rearrange("p (t s) -> p t s", t=NT),
                                             AX_X, ALU.max))
                nc.vector.tensor_scalar(xst[:, 0, h, :], xst[:, 2, h, :], -X_DH ** -0.5, None, ALU.mult)\
                  .then_inc(xm_ready, 1)
            for h in range(X_HEADS):
                dve.wait_ge(xe_ready, h + 1)
                link(nc.vector.reciprocal(xst[:, 2, h, :], xst[:, 1, h, :]))
                for t in range(NT):
                    last = nc.vector.tensor_scalar(px[:, h, t, :], px[:, h, t, :], xst[:, 2, h, t:t + 1], None, ALU.mult)
                last.then_inc(xp_ready, 1)
            dve.wait_ge(xo_hi, 1)
            nc.vector.tensor_tensor(ffT_lo[:, OX:OX + 4, :], turn[0], ffT_hi[:, OX:OX + 4, :].bitcast(F32),
                                    ALU.subtract).then_inc(xo_lo, 1)
            for n in range(D_CHUNKS):
                for j in range(U_XOG):
                    step(U_XO + U_XOG * n + j)
                dve.wait_ge(unit_done, U_XO + U_XOG * (n + 1))
                residual(pair[(n + 1) % 2], n, 1.0)
                if n:
                    take(B_F2N + n - 1, 0, xT_lo, 4 * (n - 1), xT_hi, 4 * (n - 1), V_F2 + 4 * (n - 1))

            ffn_up(U_GU2, N_F2, B_H2, B_F2N + 3, V_F2, FF_CHUNKS, 20)
            ffn_down(U_DN2, B_H2, None, None)
            variance(N_FIN, 24)
            inverse(N_FIN)
            dve.wait_ge(fn_loaded, 16)
            for t in range(NT):
                nc.vector.scalar_tensor_tensor(out=x[:, t, :], in0=x[:, t, :], scalar=rstd[:, N_FIN, t:t + 1],
                                               in1=fnorm[:], op0=ALU.mult, op1=ALU.mult).then_inc(out_ready, 1)

        @block.tensor
        def _(pe):
            def unit(u, slot, hi, khi, lo, klo, dst, width, first, last):
                pe.wait_ge(w_lo_ready, u + 1)
                for kk in range(KT_U):
                    for t in range(NT):
                        ts = slice(t * P, (t + 1) * P)
                        passes = ((hi[:, khi + kk, ts], w_hi), (hi[:, khi + kk, ts], w_lo), (lo[:, klo + kk, ts], w_hi))
                        for n, (act_t, w) in enumerate(passes):
                            mm = nc.tensor.matmul(dst[:, t, 0:width], act_t, w[:, slot, kk, 0:width],
                                                  start=(first and kk == 0 and n == 0),
                                                  stop=(last and kk == KT_U - 1 and n == 2))
                mm.then_inc(unit_done, 1)

            def batch(b, pos, src, wait_taken=True):
                if wait_taken:
                    pe.wait_ge(turn_lo, b)
                for j in range(4):
                    for t in range(NT):
                        tr = nc.tensor.transpose(turn[pos][:, j, t * P:(t + 1) * P], src(j, t), ident[:])
                tr.then_inc(turned, 1)

            def x_tiles(n):
                return lambda j, t: x[:, t, (4 * n + j) * P:(4 * n + j + 1) * P]

            pe.wait_ge(const_loaded, 16 * 17)
            nc.tensor.transpose(psum[:, 7, 0:V_ROWS], vec_rows[0:V_ROWS, :], ident[0:V_ROWS, 0:V_ROWS])\
              .then_inc(vec_turned, 1)
            for n in range(4):
                pe.wait_ge(mem_loaded[n], 16)
                if n == 1:
                    pe.wait_ge(vec_ready, 1)
                if n >= 2:
                    pe.wait_ge(turn_lo, B_MEM + n - 1)
                batch(B_MEM + n, n % 2, lambda j, t: mem_x[:, t, (4 * n + j) * P:(4 * n + j + 1) * P], False)
            for g, u0 in enumerate((U_MEMK, U_MEMV)):
                for j in range(U_G):
                    if g == 0 and j % 2 == 0:
                        pe.wait_ge(turn_lo, B_MEM + j // 2 + 1)
                    unit(u0 + j, (u0 + j) % SLOTS, ffT_hi, MEM_T + 2 * j, ffT_lo, MEM_T + 2 * j, pair[g], NW,
                         j == 0, j == U_G - 1)
                    if g == 1 and j == 1:
                        pe.wait_ge(kv_taken, 1)
                        batch(B_KX, 0, lambda h, t: hb[:, t, h * P:(h + 1) * P])
                    if g == 1 and 2 <= j < 6:
                        pe.wait_ge(x_loaded[j - 2], 16)
                        batch(B_X + j - 2, (j - 1) % 2, x_tiles(j - 2))

            def ffn_up(u0, b_x, b_h, b_x3, free_a, free_b, base_c):
                def body(ch, first):
                    for k in range(2 * U_G):
                        g, j = k // U_G, k % U_G
                        if first and g == 0 and j % 2 == 0:
                            pe.wait_ge(turn_lo, b_x + j // 2 + 1)
                        if k == 0:
                            pe.wait_ge(*free_a) if first else pe.wait_ge(gate_ready, base_c + ch)
                        if k == U_G:
                            pe.wait_ge(*free_b) if first else pe.wait_ge(h_ready, base_c + ch)
                        unit(u0 + 2 * U_G * ch + k, (u0 + k) % SLOTS, xT_hi, 2 * j, xT_lo, 2 * j, pair[g], NW,
                             j == 0, j == U_G - 1)
                        if k == 3:
                            if not first:
                                pe.wait_ge(h_ready, base_c + ch)
                                batch(b_h - 1 + ch, 0, lambda j, t: hb[:, t, j * P:(j + 1) * P])
                            elif b_x3 is not None:
                                pe.wait_ge(x_ready, 12)
                                batch(b_x3, 0, x_tiles(3))

                body(0, True)
                with pe.Fori(1, FF_CHUNKS) as ch:
                    body(ch, False)

            def ffn_down(u0, b_h, b_x, base_c, xr):
                for n in range(D_CHUNKS):
                    for k in range(U_D):
                        if n == 0 and k == 0:
                            pe.wait_ge(gate_ready, base_c + FF_CHUNKS)
                        if n == 1 and k == 0:
                            pe.wait_ge(h_ready, base_c + FF_CHUNKS)
                        if n >= 2 and k == 0:
                            pe.wait_ge(x_ready, xr + n - 1)
                        if n == 0 and k == U_D - 2:
                            pe.wait_ge(turn_lo, b_h + FF_CHUNKS)
                        u = u0 + U_D * n + k
                        unit(u, u % SLOTS, ffT_hi, 2 * k, ffT_lo, 2 * k, pair[n % 2], NW, k == 0, k == U_D - 1)
                        if k == 3:
                            if n == 0:
                                pe.wait_ge(h_ready, base_c + FF_CHUNKS)
                                batch(b_h + FF_CHUNKS - 1, 0, lambda j, t: hb[:, t, j * P:(j + 1) * P])
                            elif b_x is not None:
                                pe.wait_ge(x_ready, xr + n)
                                batch(b_x + n - 1, 0, x_tiles(n - 1))

            ffn_up(U_GU1, B_X, B_H1, None, (kv_taken, 1), (kv_taken, 2), 0)
            ffn_down(U_DN1, B_H1, B_MIXN, 0, 0)

            for n, (c0, width) in enumerate(IN_GROUPS):
                if n < 2:
                    pe.wait_ge(x_ready, 3 + n)
                else:
                    pe.wait_ge(z_ready, n - 1)
                for j in range(U_G):
                    if n == 0 and j % 2 == 0:
                        pe.wait_ge(turn_lo, B_MIXN + j // 2 + 1)
                    u = U_IN + U_G * n + j
                    unit(u, u % SLOTS, xT_hi, 2 * j, xT_lo, 2 * j, pair[n % 2], width, j == 0, j == U_G - 1)
                    if n == 0 and j == 3:
                        pe.wait_ge(x_ready, 4)
                        batch(B_MIXN + 3, 0, x_tiles(3))

            pe.wait_ge(roped, 1)
            for b in range(2):
                for j in range(4):
                    for t in range(NT):
                        tr = nc.tensor.transpose(turn[b][:, j, t * P:(t + 1) * P],
                                                 z_n[:, t, (4 * b + j) * P:(4 * b + j + 1) * P], ident[:])
                tr.then_inc(q_turned, 1)
            pe.wait_ge(q_taken, 1)
            for b in range(2):
                for g in range(NSA_KV):
                    for t in range(NT):
                        k0 = C_KV + 256 * (b + 1) + g * DH
                        for half in range(2):
                            mm = nc.tensor.matmul(turn[0][half * DH:(half + 1) * DH, 2 * b + g, t * P:(t + 1) * P],
                                                  z_n[:, t, k0:k0 + DH], ident[:], start=True, stop=True)
            mm.then_inc(k_turned, 1)
            pe.wait_ge(q_taken, 2)
            for xk in range(2):
                for g in range(NSA_KV):
                    for t in range(NT):
                        for par in range(2):
                            c0 = (2 * xk + g) * P + t * (P // 2)
                            k0 = C_KV + xk * 128 + g * DH
                            mm = nc.tensor.matmul(psum[par * DH:(par + 1) * DH, 6, c0:c0 + P // 2],
                                                  z_n[:, t, k0:k0 + DH], ident[:, par::2], start=True, stop=True)
            mm.then_inc(tok_turned, 1)
            pe.wait_ge(blk_lo_ready, 1)
            pe.wait_ge(z_ready, len(IN_GROUPS) - 1)
            for j in range(U_G):
                u = U_CMP + j
                pe.wait_ge(w_lo_ready, u + 1)
                for kk in range(KT_U):
                    for n, (tok, w) in enumerate(((blk_hi, w_hi), (blk_hi, w_lo), (blk_lo, w_hi))):
                        mm = nc.tensor.matmul(psum[0:66, 0, :], tok[:, 2 * j + kk, :], w[:, u % SLOTS, kk, :],
                                              start=(j == 0 and kk == 0 and n == 0),
                                              stop=(j == U_G - 1 and kk == KT_U - 1 and n == 2))
                mm.then_inc(unit_done, 1)
            pe.wait_ge(hid_ready, 1)
            pe.wait_ge(k_taken, 1)
            for k in range(2):
                tr = nc.tensor.transpose(psum[:, 4, k * 64:(k + 1) * 64], hid[0:64, k * P:(k + 1) * P], ident[0:64, 0:64])
            tr.then_inc(hid_turned, 1)
            pe.wait_ge(hidT_ready, 1)
            for half in range(2):
                for k in range(2):
                    nc.tensor.matmul(psum[half * DH:(half + 1) * DH, 5, 0:32], w2[:, 0, k, :], hidT[:, k, 0:32],
                                     start=(k == 0), stop=(k == 1))
            for g in range(NSA_KV):
                for k in range(2):
                    mm = nc.tensor.matmul(psum[0:REP * N_CMP, 5, 64 + g * DH:64 + (g + 1) * DH], hid_rep[:, k, g, :],
                                          w2[:, 1, k, :], start=(k == 0), stop=(k == 1))
            mm.then_inc(kvc_done, 1)
            pe.wait_ge(kvc_ready, 1)
            for t in range(NT):
                for h in range(NSA_HEADS):
                    r = slice((h % 2) * DH, (h % 2 + 1) * DH)
                    c0 = (t * REP + h // 2) * N_CMP
                    mm = nc.tensor.matmul(psum[:, 6 + h % 2, c0:c0 + N_CMP], qT[r, h // 2, t * P:(t + 1) * P],
                                          kcT[r, (h // REP) * CPAD:(h // REP) * CPAD + N_CMP], start=True, stop=True)
                mm.then_inc(sc_done, 1)
            for t in range(NT):
                pe.wait_ge(pc_ready, t + 1)
                for g in range(NSA_KV):
                    n_rows = REP * N_CMP
                    tr = nc.tensor.transpose(psum[0:n_rows, 6, (2 * t + g) * P:(2 * t + g + 1) * P],
                                             pc[:, t, g * n_rows:(g + 1) * n_rows], ident[:])
            tr.then_inc(pc_turned, 1)

            def scores(i):
                t, h0 = i // 8, 2 * (i % 8)
                w = P if t == 0 else 2 * P
                if i:
                    pe.wait_ge(s_taken, i)
                for hh in range(2):
                    h = h0 + hh
                    r = slice((h % 2) * DH, (h % 2 + 1) * DH)
                    for b in range(2):
                        mm = nc.tensor.matmul(psum[:, 4 + hh, b * w:(b + 1) * w], qT[r, h // 2, t * P:(t + 1) * P],
                                              kT[r, b, h // REP, 0:w], start=True, stop=True)
                mm.then_inc(s_done, 1)

            def turn_p(m):
                i, hh = m // 2, m % 2
                w = P if i < 8 else 2 * P
                pe.wait_ge(p_ready, i + 1)
                if m == 0:
                    pe.wait_ge(pcT_ready, 1)
                else:
                    pe.wait_ge(pT_ready, m)
                for k in range(2 * w // P):
                    tr = nc.tensor.transpose(psum[:, 6, k * P:(k + 1) * P], prob[i % 2][:, hh, k * P:(k + 1) * P], ident[:])
                tr.then_inc(p_turned, 1)

            def values(m):
                i, hh = m // 2, m % 2
                t, h = i // 8, 2 * (i % 8) + hh
                g, r = h // REP, h % REP
                nk = 1 if t == 0 else 2
                k = 2 * t + g
                pe.wait_ge(pT_ready, m + 1)
                if r == 0:
                    if k:
                        pe.wait_ge(o_taken, k)
                    nc.tensor.matmul(psum[:, 7, :], pcT[0:REP * N_CMP, t, g, :], v_blk[0:REP * N_CMP, g, :],
                                     start=True, stop=False,
                                     skip_group_check=True)
                for b in range(2):
                    for kk in range(nk):
                        c0 = C_KV + 256 * (b + 1) + 128 + g * DH
                        mm = nc.tensor.matmul(psum[:, 7, r * DH:(r + 1) * DH], probT[:, m % 2, (b * nk + kk) * P:(b * nk + kk + 1) * P],
                                              z_n[:, kk, c0:c0 + DH], start=False,
                                              stop=(r == REP - 1 and b == 1 and kk == nk - 1), skip_group_check=True)
                mm.then_inc(pv_done, 1)

            for i in range(17):
                if i < 16:
                    scores(i)
                if i >= 1:
                    for m in (2 * i - 2, 2 * i - 1):
                        turn_p(m)
                        if m:
                            values(m - 1)
            values(31)

            for b in range(2):
                if b == 1:
                    pe.wait_ge(o_taken, 4)
                for j in range(4):
                    for t in range(NT):
                        c0 = HG_W + (4 * b + j) * HG_D
                        tr = nc.tensor.transpose(turn[b][:, j, t * P:(t + 1) * P], z_qf[:, t, c0:c0 + HG_D], ident[:])
                tr.then_inc(f_turned, 1)
            for b in range(2):
                pe.wait_ge(f_sig, b + 1)
                for j in range(4):
                    for t in range(NT):
                        c0 = (4 * b + j) * HG_D
                        tr = nc.tensor.transpose(turn[b][:, j, t * P:(t + 1) * P], z_qf[:, t, c0:c0 + HG_D], ident[:])
                tr.then_inc(hq_turned, 1)
            pe.wait_ge(kf_ready, 1)
            pe.wait_ge(hq_taken, 2)
            for b in range(4):
                for hh in range(2):
                    for t in range(NT):
                        h, ts = 2 * b + hh, slice(t * P, (t + 1) * P)
                        mm = nc.tensor.matmul(psum[:, 4 + b, (2 * hh + t) * P:(2 * hh + t + 1) * P], kgT[:, h, ts],
                                              qfT[:, h, ts], start=True, stop=True)
                mm.then_inc(dg_done, 1)
            for l, m in enumerate(LEVELS):
                pe.wait_ge(qk_ready, l + 1)
                for half in range(2):
                    n = 2 * l + half
                    if n < 4:
                        pe.wait_ge(dg_taken, n + 1)
                    else:
                        pe.wait_ge(lv_taken, n - 3)
                    for hh in range(4):
                        h = 4 * half + hh
                        for t in range(NT):
                            q_late = qfT[:, h, t * P:(t + 1) * P].rearrange("p (b x m) -> p b x m", x=2, m=m)[:, :, 1, :]
                            c0 = (2 * hh + t) * (P // 2)
                            mm = nc.tensor.matmul(
                                psum[:, 4 + n % 4, c0:c0 + P // 2].rearrange("p (b m) -> p b m", m=m),
                                kgT[:, h, t * P:(t + 1) * P], q_late, start=True, stop=True)
                    mm.then_inc(lv_done, 1)
            pe.wait_ge(qk_ready, len(LEVELS) + 1)
            pe.wait_ge(lv_taken, 2 * len(LEVELS))
            for h in range(HG_HEADS):
                mm = nc.tensor.matmul(psum[:, 4 + h // 4, (h % 4) * P:(h % 4 + 1) * P], kgT[:, h, 0:P],
                                      qfT[:, h, P:SEQ], start=True, stop=True)
            mm.then_inc(cross_done, 1)
            pe.wait_ge(cross_taken, 1)
            for t in range(NT):
                for h in range(HG_HEADS):
                    dst = psum[:, 4 + 2 * t + h // 4, (h % 4) * P:(h % 4 + 1) * P]
                    vs = slice(h * HG_D, (h + 1) * HG_D)
                    mm = nc.tensor.matmul(dst, att[:, h, t, :], z_ig[:, t, vs], start=True, stop=(t == 0))
                    if t == 1:
                        mm = nc.tensor.matmul(dst, att_x[:, h, :], z_ig[:, 0, vs], start=False, stop=True)
                mm.then_inc(ho_done, 1)
            pe.wait_ge(mix_ready, 1)
            for n in range(4):
                if n >= 2:
                    pe.wait_ge(turn_lo, B_MIX + n - 1)
                if n < 2:
                    batch(B_MIX + n, n % 2,
                          lambda j, t: z_ig[:, t, HG_W + (4 * n + j) * P:HG_W + (4 * n + j + 1) * P], False)
                else:
                    batch(B_MIX + n, n % 2, lambda j, t: z_n[:, t, (4 * n - 8 + j) * P:(4 * n - 7 + j) * P], False)

            for n in range(D_CHUNKS):
                if n == 0:
                    pe.wait_ge(hid_ready, 1)
                elif n == 1:
                    pe.wait_ge(z_ready, len(IN_GROUPS))
                else:
                    pe.wait_ge(x_ready, 4 + n - 1)
                for j in range(U_G):
                    if n == 0 and j % 2 == 0:
                        pe.wait_ge(turn_lo, B_MIX + j // 2 + 1)
                    u = U_OUT + U_G * n + j
                    unit(u, u % SLOTS, ffT_hi, MIX_HI + 2 * j, ffT_lo, MIX_LO + 2 * j, pair[n % 2], NW,
                         j == 0, j == U_G - 1)
                    if j == 3 and n:
                        pe.wait_ge(x_ready, 4 + n)
                        batch(B_XAN + n - 1, 0, x_tiles(n - 1))
            pe.wait_ge(x_ready, 4 + 3)
            for j in range(U_G):
                if j % 2 == 0:
                    pe.wait_ge(turn_lo, B_XAN + j // 2 + 1)
                u = U_XQ + j
                unit(u, u % SLOTS, xT_hi, 2 * j, xT_lo, 2 * j, pair[0], NW, j == 0, j == U_G - 1)
                if j == 3:
                    pe.wait_ge(x_ready, 8)
                    batch(B_XAN + 3, 0, x_tiles(3))
            pe.wait_ge(qx_ready, 1)
            for h in range(X_HEADS):
                for t in range(NT):
                    tr = nc.tensor.transpose(turn[0][:, h, t * P:(t + 1) * P], qx[:, t, h * X_DH:(h + 1) * X_DH], ident[:])
            tr.then_inc(qx_turned, 1)
            pe.wait_ge(qx_taken, 1)
            for h in range(X_HEADS):
                for t in range(NT):
                    mm = nc.tensor.matmul(psum[:, 4 + h, t * MEM:(t + 1) * MEM], qxT[:, h, t * P:(t + 1) * P],
                                          kxT[:, h, :], start=True, stop=True)
                mm.then_inc(xs_done, 1)
            for h in range(X_HEADS):
                pe.wait_ge(xp_ready, h + 1)
                for k in range(MEM // P):
                    for t in range(NT):
                        tr = nc.tensor.transpose(psum[:, 4 + h, k * SEQ + t * P:k * SEQ + (t + 1) * P],
                                                 px[:, h, t, k * P:(k + 1) * P], ident[:])
                tr.then_inc(xp_turned, 1)
            for h in range(X_HEADS):
                if h == 0:
                    pe.wait_ge(xpT_ready, 2)
                else:
                    pe.wait_ge(xpT_ready, h + 1)
                for k in range(MEM // P):
                    mm = nc.tensor.matmul(turn[0][:, h, :], vx[:, k, h * X_DH:(h + 1) * X_DH], pxT[:, h, k, :],
                                          start=(k == 0), stop=(k == 1))
            mm.then_inc(xo_done, 1)
            pe.wait_ge(xo_lo, 1)
            for n in range(D_CHUNKS):
                if n == 0:
                    pe.wait_ge(x_ready, 8)
                elif n == 1:
                    pe.wait_ge(qx_ready, 1)
                else:
                    pe.wait_ge(x_ready, 8 + n - 1)
                for j in range(U_XOG):
                    u = U_XO + U_XOG * n + j
                    unit(u, u % SLOTS, ffT_hi, OX + 2 * j, ffT_lo, OX + 2 * j, pair[(n + 1) % 2], NW,
                         j == 0, j == U_XOG - 1)
                if n:
                    pe.wait_ge(x_ready, 8 + n)
                    batch(B_F2N + n - 1, 0, x_tiles(n - 1), n > 1)

            ffn_up(U_GU2, B_F2N, B_H2, B_F2N + 3, (x_ready, 12), (x_ready, 11), FF_CHUNKS)
            ffn_down(U_DN2, B_H2, None, FF_CHUNKS, 12)


def constants():
    import numpy as np
    tok = np.arange(P)
    end = np.arange(N_CMP) * CMP_STRIDE + CMP_LEN - 1
    valid = end[None, None, :] <= (tok[:, None, None] + P * np.arange(NT)[None, :, None])
    key = np.arange(SEQ)
    causal = np.where(key[None, :] <= tok[:, None] + P, 0.0, NEG)
    masks = np.zeros((P, len(LEVELS), P // 2), np.float32)
    for l, m in enumerate(LEVELS):
        late = (np.arange(P // (2 * m))[:, None] * 2 * m + m + np.arange(m)[None, :]).ravel()
        hit = (tok[:, None] // (2 * m) == late[None, :] // (2 * m)) & (tok[:, None] % (2 * m) < m)
        masks[:, l, :] = hit
    blk = (tok[:, None] // N_CMP == np.arange(REP)[None, :]).astype(np.float32)
    half = DH // 2
    inv = 10000.0 ** (-np.arange(half, dtype=np.float64) / half)
    return {
        "ident": np.eye(P, dtype=np.float32),
        "inv_f": np.broadcast_to(inv.astype(np.float32), (P, half)).copy(),
        "causal": causal.astype(np.float32),
        "cmp_add": np.where(valid, 0.0, NEG).astype(np.float32),
        "cmp_mul": valid.astype(np.float32),
        "diag_blk": blk,
        "lvl_mask": masks,
    }


def kernel(**inputs):
    import numpy as np
    import concourse.bacc as bacc
    from concourse.bass_utils import run_bass_kernel_spmd

    nc = bacc.Bacc("TRN2", target_bir_lowering=False, num_devices=1)
    laid = {
        "x": inputs["x"][0], "mem": inputs["mem"][0], "pos": inputs["positions"][0],
        "n1": inputs["ffn1_norm"][0], "g1": inputs["ffn1_w_gate"][0], "u1": inputs["ffn1_w_up"][0],
        "d1": inputs["ffn1_w_down"][0], "nm": inputs["mix_norm"][0], "w_in": inputs["w_in"][0],
        "lb": inputs["hgrn_lb_logits"].reshape(-1), "nhg": inputs["hgrn_out_norm"][0],
        "pe": inputs["nsa_cmp_pe"][0].reshape(-1),
        "cw1": np.concatenate([inputs["nsa_cmp_k_w1"][0], inputs["nsa_cmp_v_w1"][0]], axis=1),
        "kw2": inputs["nsa_cmp_k_w2"][0], "vw2": inputs["nsa_cmp_v_w2"][0],
        "w_out": inputs["w_out"][0], "nx": inputs["xattn_norm"][0], "nmem": inputs["mem_norm"][0],
        "wq": inputs["xattn_wq"][0], "wk": inputs["xattn_wk"][0], "wv": inputs["xattn_wv"][0],
        "wo": inputs["xattn_wo"][0], "n2": inputs["ffn2_norm"][0], "g2": inputs["ffn2_w_gate"][0],
        "u2": inputs["ffn2_w_up"][0], "d2": inputs["ffn2_w_down"][0], "fn": inputs["final_norm"],
    }
    arrays, given, tables = {}, {}, {}
    for name, value in laid.items():
        arrays["in_" + name] = np.ascontiguousarray(value)
        given[name] = nc.dram_tensor("in_" + name, arrays["in_" + name].shape,
                                     mybir.dt.from_np(arrays["in_" + name].dtype), kind="ExternalInput").ap()
    for name, value in constants().items():
        arrays["c_" + name] = value
        tables[name] = nc.dram_tensor("c_" + name, value.shape, mybir.dt.from_np(value.dtype),
                                      kind="ExternalInput").ap()
    out = nc.dram_tensor("out", (SEQ, D), F32, kind="ExternalOutput").ap()
    layer_program(nc, given, tables, out)
    r = run_bass_kernel_spmd(nc, [arrays], core_ids=[0])
    return r.results[0]["out"].reshape(1, SEQ, D)
```

```python
from contextlib import ExitStack

import concourse.bass as bass
from concourse import mybir

P = 128
F32 = mybir.dt.float32
F32R = mybir.dt.float32r
I32 = mybir.dt.int32
U8 = mybir.dt.uint8
ALU = mybir.AluOpType
ACT = mybir.ActivationFunctionType
AX_X = mybir.AxisListType.X

D = 2048
SEQ = 256
NT = SEQ // P
MEM = 256
EPS = 1e-6
D_FF = 5632
HG_HEADS, HG_D = 8, 128
HG_W = HG_HEADS * HG_D
NSA_HEADS, NSA_KV, DH = 16, 2, 64
REP = NSA_HEADS // NSA_KV
CMP_LEN, CMP_STRIDE, CMP_HIDDEN = 32, 16, 256
N_CMP = (SEQ - CMP_LEN) // CMP_STRIDE + 1
CPAD = 16
X_HEADS, X_DH = 4, 128
D_IN = 4 * HG_W + NSA_HEADS * DH + 6 * NSA_KV * DH + NSA_HEADS * 3
C_NSA = 4 * HG_W
C_KV = NSA_HEADS * DH
C_GATE = C_KV + 6 * NSA_KV * DH
W_NSA = C_GATE + NSA_HEADS * 3
NEG = -1e30
TWO_PI = 6.283185307179586
PI_A = 6.28125
PI_B = 0.00193500518798828125
PI_C = TWO_PI - PI_A - PI_B
ROUND = 12582912.0

NW = 512
KT_U = 2
SLOTS = 4
KD = D // P
KF = D_FF // P
U_G = KD // KT_U
U_D = KF // KT_U
FF_CHUNKS = D_FF // NW
D_CHUNKS = D // NW
IN_GROUPS = ([(C_NSA + C_KV, NW), (C_NSA + C_KV + NW, D_IN - C_NSA - C_KV - NW),
              (C_NSA, NW), (C_NSA + NW, NW)]
             + [(c, NW) for c in (1024, 1536, 0, 512, 2048, 2560, 3072, 3584)])
U_MEMK = 0
U_MEMV = U_MEMK + U_G
U_GU1 = U_MEMV + U_G
U_DN1 = U_GU1 + 2 * U_G * FF_CHUNKS
U_IN = U_DN1 + U_D * D_CHUNKS
CMP = -1
MID = ([(g, j) for g in range(5) for j in range(U_G)] + [(5, j) for j in range(6)]
       + [(CMP, j) for j in range(U_G)] + [(5, j) for j in range(6, U_G)]
       + [(g, j) for g in range(6, len(IN_GROUPS)) for j in range(U_G)])
OUT_ORDER = (6, 7, 4, 5, 0, 1, 2, 3)
U_CMP = U_IN + MID.index((CMP, 0))
U_OUT = U_IN + len(MID)
FILL_ROPE, FILL_ROPED, FILL_Q, FILL_K, FILL_CMP = 1, 2, 2, 2, U_G
FILL_HID, FILL_KV, FILL_SC, FILL_PC = 2, 2, 2, 4
_LEFT = (len(MID) - 4 * U_G - 8 * FILL_ROPE - FILL_ROPED - FILL_Q - FILL_K - FILL_CMP - FILL_HID - FILL_KV - FILL_SC
         - FILL_PC)
SLOTS_U, SLOTS_ALL = 22, 36
ITEM_UNITS = [_LEFT * (i + 1) // SLOTS_U - _LEFT * i // SLOTS_U for i in range(SLOTS_U)]
HG_STEPS = 3 + 2 * 7
assert U_IN + 4 * U_G + 8 * FILL_ROPE + FILL_ROPED + FILL_Q + FILL_K == U_CMP
U_XQ = U_OUT + U_G * D_CHUNKS
U_XO = U_XQ + U_G
U_XOG = X_HEADS // KT_U
U_GU2 = U_XO + U_XOG * D_CHUNKS
U_DN2 = U_GU2 + 2 * U_G * FF_CHUNKS
U_END = U_DN2 + U_D * D_CHUNKS

B_MEM = 0
B_X = B_MEM + 4
B_KX = B_X + 4
B_H1 = B_KX + 1
B_MIXN = B_H1 + FF_CHUNKS
B_MIX = B_MIXN + 4
B_XAN = B_MIX + 4
B_F2N = B_XAN + 4
B_H2 = B_F2N + 4

V_F1, V_MIX, V_XA, V_MEM, V_F2, V_LB, V_PE, V_HG = 0, 16, 32, 48, 64, 80, 96, 112
V_ROWS = 120
N_MEM, N_F1, N_MIX, N_XA, N_F2, N_FIN = range(6)
LEVELS = [1, 2, 4, 8, 16, 32, 64]


def layer_program(nc, a, c, out):
    with ExitStack() as ctx:
        def sem(name):
            return ctx.enter_context(nc.semaphore(name))

        arena = ctx.enter_context(nc.sbuf_tensor("arena", [P, 206 * 1024], U8))
        base = (nc.sbuf_base - 206 * 1024 + 63) // 64 * 64
        at = [base]

        def put(name, shape, dt, size=4):
            n = size
            for s in shape[1:]:
                n *= s
            t = nc.alloc_sbuf_tensor_at(name, shape, dt, offset=at[0])
            at[0] += (n + 31) // 32 * 32
            return t

        x = put("x", [P, NT, D], F32)
        at_xT = [at[0]]
        xT_hi = put("xT_hi", [P, KD, SEQ], F32R)
        xT_lo = put("xT_lo", [P, KD, SEQ], F32R)
        xt_end = at[0]
        w_raw = put("w_raw", [P, SLOTS, KT_U, NW], F32)
        w_hi = put("w_hi", [P, SLOTS, KT_U, NW], F32R)
        w_lo = put("w_lo", [P, SLOTS, KT_U, NW], F32R)
        sg = put("silu_gate", [P, NT, NW], F32)
        hb = put("ff_hidden", [P, NT, NW], F32)
        keep = at[0]
        kxT = put("kxT", [P, X_HEADS, MEM], F32)
        vx = put("vx", [P, MEM // P, X_HEADS * X_DH], F32)
        fnorm = nc.alloc_sbuf_tensor_at("final_norm_rows", [P, D], F32, offset=keep)
        ident = put("ident", [P, P], F32)
        causal = put("causal", [P, SEQ], F32)
        cmp_add = put("cmp_add", [P, NT, N_CMP], F32)
        cmp_mul = put("cmp_mul", [P, NT, N_CMP], F32)
        diag_blk = put("diag_blk", [P, REP], F32)
        inv_f = put("inv_f", [P, DH // 2], F32)
        pos_i = put("pos_i", [P, NT], I32)
        pos_f = put("pos_f", [P, NT], F32)
        vec = put("vec", [P, V_ROWS], F32)
        sin_t = put("sin_t", [P, NT, DH // 2], F32)
        cos_t = put("cos_t", [P, NT, DH // 2], F32)
        ss = put("ss", [P, 6, NT, 4], F32)
        var = put("var", [P, 6, NT], F32)
        std = put("std", [P, 6, NT], F32)
        rstd = put("rstd", [P, 6, NT], F32)
        lb_w = put("lb_w", [P, 5, HG_HEADS], F32)
        w2 = put("w2", [P, 2, 2, DH], F32)
        ff = at[0]
        ffT_hi = put("ffT_hi", [P, KF, SEQ], F32R)
        ffT_lo = put("ffT_lo", [P, KF, SEQ], F32R)
        ff_end = at[0]
        assert ff_end <= base + 206 * 1024, ff_end - base

        def place(name, shape, off, dt=F32):
            n = 1 if dt == U8 else 4
            for s in shape[1:]:
                n *= s
            assert ff + off + n <= ff_end, name
            return nc.alloc_sbuf_tensor_at(name, shape, dt, offset=ff + off)

        mem_x = place("mem_x", [P, NT, D], 0)
        vec_rows = place("vec_rows", [P, P], 16384)
        ang = place("ang", [P, 4, NT, DH // 2], 16896)
        z_qf = place("z_qf", [P, NT, 2 * HG_W], 0)
        z_ig = place("z_ig", [P, NT, 2 * HG_W], 16384)
        z_n = place("z_n", [P, NT, W_NSA], 32768)
        o1 = 32768 + 4 * NT * W_NSA
        qT = place("qT", [P, REP, SEQ], o1)
        kT = place("kT", [P, 2, NSA_KV, SEQ], o1 + 8192)
        rtmp = place("rtmp", [P, 4, NSA_HEADS * DH // 2], o1 + 12288)
        blk = place("blk", [P, KD, 66], o1 + 12288)
        blk_hi = place("blk_hi", [P, KD, 66], o1 + 16640, F32R)
        blk_lo = place("blk_lo", [P, KD, 66], o1 + 20992, F32R)
        o2 = o1 + 25344
        hid = place("hid", [P, CMP_HIDDEN], o2)
        hidT = place("hidT", [P, 2, 64], o2 + 1024)
        hid_rep = place("hid_rep", [P, 2, NSA_KV, REP * N_CMP], o2 + 1536)
        kcT = place("kcT", [P, 32], o2 + 3456)
        v_blk = place("v_blk", [P, NSA_KV, REP * DH], o2 + 3584)
        gate = place("gate", [P, NT, NSA_HEADS, 3], o2 + 7680)
        mx = place("mx", [P, NT, NSA_HEADS, 2], o2 + 8064)
        sm = place("sm", [P, NT, NSA_HEADS, 2], o2 + 8320)
        rc = place("rc", [P, NT, NSA_HEADS, 2], o2 + 8576)
        cstat = place("cstat", [P, NT, 2, NSA_HEADS], o2 + 8832)
        pc = place("pc", [P, NT, NSA_HEADS * N_CMP], o2 + 9088)
        pcT = place("pcT", [P, NT, NSA_KV, P], o2 + 11008)
        prob = [place("prob0", [P, 2, 512], o1 + 12288), place("prob1", [P, 2, 512], o1 + 16640),
                sg]
        probT = place("probT", [P, 2, 512], o1 + 20992)
        xt = at_xT

        def place_xt(name, shape):
            n = 4
            for d in shape[1:]:
                n *= d
            t_ = nc.alloc_sbuf_tensor_at(name, shape, F32, offset=xt[0])
            xt[0] += n
            assert xt[0] <= xt_end, name
            return t_

        fT = place_xt("fT", [P, HG_HEADS, SEQ])
        qfT = place_xt("qfT", [P, HG_HEADS, SEQ])
        kgT = place_xt("kgT", [P, HG_HEADS, SEQ])
        tots = {1: fT}
        for m in LEVELS[1:]:
            tots[m] = place_xt(f"tot{m}", [P, HG_HEADS, SEQ // m])
        hst = place("hst", [P, 4, NT, HG_HEADS], 88576)
        att = place("att", [P, HG_HEADS, NT, P], 0)
        att_x = place("att_x", [P, HG_HEADS, P], 8192)
        lvl_f32 = place("lvl_f32", [P, len(LEVELS), P // 2], 86016)
        lvl_mask = place("lvl_mask", [P, len(LEVELS), P // 2], 88064, U8)
        qx = place("qx", [P, NT, X_HEADS * X_DH], 16384)
        qxT = place("qxT", [P, X_HEADS, SEQ], 20480)
        px = place("px", [P, X_HEADS, NT, MEM], 67584)
        pxT = place("pxT", [P, X_HEADS, MEM // P, SEQ], 24576)
        xst = place("xst", [P, 3, X_HEADS, NT], 67584 + 8192)
        MIX_HI, MIX_LO, OX = 0, 6, 40
        MEM_T = 28

        psum = ctx.enter_context(nc.psum_tensor("psum", [P, 8, 512], F32))
        pair = [psum[:, 0:2, :], psum[:, 2:4, :]]
        turn = [psum[:, 4:6, :].rearrange("p b (k t) -> p (b k) t", t=SEQ),
                psum[:, 6:8, :].rearrange("p b (k t) -> p (b k) t", t=SEQ)]
        hturn = [psum[:, 2 * b:2 * b + 2, :].rearrange("p b (k t) -> p (b k) t", t=SEQ) for b in range(2)]

        w_loaded = [sem(f"w_loaded{i}") for i in range(SLOTS)]
        w_hi_ready = sem("w_hi_ready")
        w_lo_ready = sem("w_lo_ready")
        unit_done = sem("unit_done")
        turned = sem("turned")
        turn_hi = sem("turn_hi")
        turn_lo = sem("turn_lo")
        const_loaded = sem("const_loaded")
        vec_loaded = sem("vec_loaded")
        mask_loaded = sem("mask_loaded")
        mem_loaded = [sem(f"mem_loaded{i}") for i in range(4)]
        x_loaded = [sem(f"x_loaded{i}") for i in range(4)]
        vec_turned = sem("vec_turned")
        vec_ready = sem("vec_ready")
        sq_done = sem("sq_done")
        var_ready = sem("var_ready")
        std_ready = sem("std_ready")
        rstd_ready = sem("rstd_ready")
        trig_args = sem("trig_args")
        trig_ready = sem("trig_ready")
        lb_exp = sem("lb_exp")
        kv_taken = sem("kv_taken")
        gate_ready = sem("gate_ready")
        h_ready = sem("h_ready")
        x_ready = sem("x_ready")
        z_ready = sem("z_ready")
        dve_step = sem("dve_step")
        act_step = sem("act_step")
        roped = sem("roped")
        q_turned = sem("q_turned")
        q_taken = sem("q_taken")
        k_turned = sem("k_turned")
        k_taken = sem("k_taken")
        tok_turned = sem("tok_turned")
        blk_ready = sem("blk_ready")
        blk_hi_ready = sem("blk_hi_ready")
        blk_lo_ready = sem("blk_lo_ready")
        hid_ready = sem("hid_ready")
        hid_turned = sem("hid_turned")
        hidT_ready = sem("hidT_ready")
        kvc_done = sem("kvc_done")
        kvc_ready = sem("kvc_ready")
        sc_done = sem("sc_done")
        sc_ready = sem("sc_ready")
        ec_ready = sem("ec_ready")
        pc_ready = sem("pc_ready")
        pc_turned = sem("pc_turned")
        pcT_ready = sem("pcT_ready")
        gates_ready = sem("gates_ready")
        s_done = sem("s_done")
        s_taken = sem("s_taken")
        e_ready = sem("e_ready")
        p_ready = sem("p_ready")
        p_turned = sem("p_turned")
        pT_ready = sem("pT_ready")
        pv_done = sem("pv_done")
        o_taken = sem("o_taken")
        f_turned = sem("f_turned")
        f_sig = sem("f_sig")
        hq_turned = sem("hq_turned")
        hq_taken = sem("hq_taken")
        kf_ready = sem("kf_ready")
        dg_done = sem("dg_done")
        dg_taken = sem("dg_taken")
        qk_ready = sem("qk_ready")
        lv_done = sem("lv_done")
        lv_taken = sem("lv_taken")
        cross_done = sem("cross_done")
        cross_taken = sem("cross_taken")
        ho_done = sem("ho_done")
        ho_sq = sem("ho_sq")
        ho_gated = sem("ho_gated")
        ho_var = sem("ho_var")
        ho_std = sem("ho_std")
        g_silu = sem("g_silu")
        mix_ready = sem("mix_ready")
        qx_ready = sem("qx_ready")
        qx_turned = sem("qx_turned")
        qx_taken = sem("qx_taken")
        xs_done = sem("xs_done")
        xm_ready = sem("xm_ready")
        xe_ready = sem("xe_ready")
        xp_ready = sem("xp_ready")
        xp_turned = sem("xp_turned")
        xpT_ready = sem("xpT_ready")
        xo_done = sem("xo_done")
        xo_hi = sem("xo_hi")
        xo_lo = sem("xo_lo")
        fn_loaded = sem("fn_loaded")
        fn_applied = sem("fn_applied")
        out_scaled = sem("out_scaled")
        out_ready = sem("out_ready")
        stored = sem("stored")

        block = ctx.enter_context(nc.Block())

        def cols(w, j, c0, width):
            return w[KT_U * P * j:KT_U * P * (j + 1), c0:c0 + width].rearrange("(k p) n -> p k n", p=P)

        def dyn_cols(w, j, chunk):
            return w[KT_U * P * j:KT_U * P * (j + 1), bass.ts(chunk, NW)].rearrange("(k p) n -> p k n", p=P)

        @block.sync
        def _(sp):
            def load(u, slot, src, first=False):
                if not first:
                    sp.wait_ge(w_lo_ready, u - (SLOTS - 1))
                sp.dma_start(w_raw[:, slot, :, 0:src.shape[2]], src).then_inc(w_loaded[slot], 16)

            for g, w in enumerate((a["wk"], a["wv"])):
                for j in range(U_G):
                    u = U_MEMK + U_G * g + j
                    load(u, u % SLOTS, cols(w, j, 0, NW), first=u < SLOTS)

            def gate_up(u0, wg, wu):
                with sp.Fori(0, FF_CHUNKS) as ch:
                    for k, w in enumerate((wg, wu)):
                        for j in range(U_G):
                            kk = U_G * k + j
                            load(u0 + 2 * U_G * ch + kk, (u0 + kk) % SLOTS, dyn_cols(w, j, ch))

            def down(u0, w):
                for n in range(D_CHUNKS):
                    for j in range(U_D):
                        u = u0 + U_D * n + j
                        load(u, u % SLOTS, cols(w, j, n * NW, NW))

            gate_up(U_GU1, a["g1"], a["u1"])
            down(U_DN1, a["d1"])
            for i, (g, j) in enumerate(MID):
                if i == 2 * U_G:
                    sp.wait_ge(z_ready, 1)
                    sp.dma_start(lvl_f32[:], c["lvl_mask"]).then_inc(mask_loaded, 16)
                src = cols(a["cw1"], j, 0, NW) if g == CMP else cols(a["w_in"], j, *IN_GROUPS[g])
                load(U_IN + i, (U_IN + i) % SLOTS, src)
            for n in range(D_CHUNKS):
                for j in range(U_G):
                    u = U_OUT + U_G * n + j
                    load(u, u % SLOTS, cols(a["w_out"], OUT_ORDER[j], n * NW, NW))
            for j in range(U_G):
                load(U_XQ + j, (U_XQ + j) % SLOTS, cols(a["wq"], j, 0, NW))
            for n in range(D_CHUNKS):
                for j in range(U_XOG):
                    u = U_XO + U_XOG * n + j
                    load(u, u % SLOTS, cols(a["wo"], j, n * NW, NW))
            gate_up(U_GU2, a["g2"], a["u2"])
            sp.wait_ge(xo_lo, 1)
            sp.dma_start(fnorm[:], a["fn"].rearrange("(o n) -> o n", o=1).broadcast_to([P, D]))\
              .then_inc(fn_loaded, 16)
            down(U_DN2, a["d2"])
            sp.wait_ge(out_ready, 1)
            sp.dma_start(out[0:P, 0:D - NW], x[:, 0, 0:D - NW]).then_inc(stored, 16)
            sp.wait_ge(out_scaled, 1)
            sp.dma_start(out[P:SEQ, 0:D - NW], x[:, 1, 0:D - NW]).then_inc(stored, 16)
            for t in range(NT):
                sp.wait_ge(out_ready, t + 2)
                sp.dma_start(out[t * P:(t + 1) * P, D - NW:], x[:, t, D - NW:]).then_inc(stored, 16)
            sp.wait_ge(stored, 16 * 4)

        @block.scalar
        def _(act):
            chain = [0]

            def link(ins):
                chain[0] += 1
                ins.then_inc(act_step, 1)
                act.wait_ge(act_step, chain[0])

            def split(u, slot, turn_no, first=False):
                act.wait_ge(w_loaded[slot], 16 * turn_no)
                if not first:
                    act.wait_ge(unit_done, u - (SLOTS - 1))
                nc.scalar.activation(w_hi[:, slot], w_raw[:, slot], ACT.Copy).then_inc(w_hi_ready, 1)

            def step(u):
                if u + SLOTS < U_END:
                    split(u + SLOTS, u % SLOTS, u // SLOTS + 2)

            mid = [0]

            def fill(n):
                for _ in range(n):
                    step(U_IN + mid[0])
                    mid[0] += 1

            def take(b, pos, dst, kt, scale=None, junk=None):
                act.wait_ge(turned, b + 1)
                if scale is None:
                    nc.scalar.activation(dst[:, kt:kt + 4, :] if isinstance(kt, int) else dst[:, bass.ts(kt[0], 4), :],
                                         turn[pos], ACT.Copy).then_inc(turn_hi, 1)
                    return
                for j in range(4):
                    last = nc.scalar.activation(dst[:, kt + j, :], turn[pos][:, j, :], ACT.Copy,
                                                scale=vec[:, scale + j:scale + j + 1])
                last.then_inc(turn_hi, 1)

            def squares(src, norm, n):
                for t in range(NT):
                    last = nc.scalar.activation(sg[:, t, :], src[:, t, n * NW:(n + 1) * NW], ACT.Square,
                                                accum_out=ss[:, norm, t, n:n + 1])
                last.then_inc(sq_done, 1)
                sq[0] += 1
                act.wait_ge(sq_done, sq[0])

            sq = [0]

            def root(norm):
                act.wait_ge(var_ready, norm + 1)
                nc.scalar.activation(std[:, norm, :], var[:, norm, :], ACT.Sqrt).then_inc(std_ready, 1)

            def load_mem(n):
                act.dma_start(mem_x[:, :, n * NW:(n + 1) * NW],
                              a["mem"][:, n * NW:(n + 1) * NW].rearrange("(t p) n -> p t n", p=P))\
                   .then_inc(mem_loaded[n], 16)

            load_mem(0)
            act.dma_start(ident[:], c["ident"]).then_inc(vec_loaded, 16)
            for r0, name, n in ((V_F1, "n1", 16), (V_MIX, "nm", 16), (V_XA, "nx", 16), (V_MEM, "nmem", 16),
                                (V_F2, "n2", 16), (V_LB, "lb", 16), (V_HG, "nhg", 8), (V_PE, "pe", 16)):
                act.dma_start(vec_rows[r0:r0 + n, :], a[name].rearrange("(r p) -> r p", p=P))\
                   .then_inc(vec_loaded, 16)
            for n in range(1, 4):
                load_mem(n)
            act.dma_start(pos_i[:], a["pos"].rearrange("(t p) -> p t", p=P), allow_slow_non_contiguous=True).then_inc(const_loaded, 16)
            for dst, name in ((inv_f, "inv_f"), (causal, "causal"), (cmp_add, "cmp_add"), (cmp_mul, "cmp_mul"),
                              (diag_blk, "diag_blk")):
                act.dma_start(dst[:], c[name]).then_inc(const_loaded, 16)
            for i, name in enumerate(("kw2", "vw2")):
                act.dma_start(w2[:, i], a[name].rearrange("(k p) n -> p k n", p=P)).then_inc(const_loaded, 16)
            for n in range(4):
                act.dma_start(x[:, :, n * NW:(n + 1) * NW],
                              a["x"][:, n * NW:(n + 1) * NW].rearrange("(t p) n -> p t n", p=P))\
                   .then_inc(x_loaded[n], 16)

            for n in range(4):
                act.wait_ge(mem_loaded[n], 16)
                squares(mem_x, N_MEM, n)
                if n == 0:
                    act.wait_ge(vec_ready, 1)
                take(B_MEM + n, n % 2, ffT_hi, MEM_T + 4 * n, V_MEM + 4 * n)
                split(n, n, 1, first=True)
            root(N_MEM)
            act.wait_ge(lb_exp, 1)
            nc.scalar.activation(lb_w[:, 2:4, :], lb_w[:, 0:2, :], ACT.Exp).then_inc(lb_exp, 1)
            for j in range(U_G):
                step(U_MEMK + j)
                if j % 2 == 1:
                    n = j // 2
                    act.wait_ge(x_loaded[n], 16)
                    squares(x, N_F1, n)
                    take(B_X + n, n % 2, xT_hi, 4 * n, V_F1 + 4 * n)
            for j in range(U_G):
                step(U_MEMV + j)
                if j == 2:
                    act.wait_ge(turned, B_KX + 1)
                    nc.scalar.activation(kxT[:, 0:2, :], turn[0][:, 0:2, :], ACT.Copy).then_inc(turn_hi, 1)
            root(N_F1)
            act.wait_ge(trig_args, 1)
            nc.scalar.activation(sin_t[:], ang[:, 1], ACT.Sin)
            nc.scalar.activation(cos_t[:], ang[:, 2], ACT.Sin).then_inc(trig_ready, 1)

            def ffn_up(u0, norm, b_h, b_x3, s_x3, base_c):
                def body(ch, first):
                    for k in range(2 * U_G):
                        u = u0 + 2 * U_G * ch + k
                        split(u + SLOTS, (u0 + k) % SLOTS, (u0 + k) // SLOTS + 2 + (2 * U_G // SLOTS) * ch)
                        if k == 4:
                            if not first:
                                take(b_h - 1 + ch, 0, ffT_hi, (ch - 1,))
                            elif b_x3 is not None:
                                squares_take3()
                        if k == U_G - 1:
                            act.wait_ge(unit_done, u + 1)
                            if first:
                                if base_c:
                                    act.wait_ge(h_ready, base_c)
                            else:
                                act.wait_ge(h_ready, base_c + ch)
                            for t in range(NT):
                                last = nc.scalar.activation(sg[:, t, :], pair[0][:, t, :], ACT.Silu,
                                                            scale=rstd[:, norm, t:t + 1])
                            last.then_inc(gate_ready, 1)

                def squares_take3():
                    take(b_x3, 0, xT_hi, 12, s_x3 + 12)
                    root(norm)
                    act.wait_ge(rstd_ready, norm + 1)

                if b_x3 is None:
                    act.wait_ge(rstd_ready, norm + 1)
                body(0, True)
                with act.Fori(1, FF_CHUNKS) as ch:
                    body(ch, False)

            def ffn_down(u0, norm, b_h, b_x, s_x, xr):
                for n in range(D_CHUNKS):
                    for k in range(U_D):
                        step(u0 + U_D * n + k)
                        if k == 4:
                            if n == 0:
                                take(b_h + FF_CHUNKS - 1, 0, ffT_hi, KF - 4)
                            elif b_x is not None:
                                take(b_x + n - 1, 0, xT_hi, 4 * (n - 1), s_x + 4 * (n - 1))
                    act.wait_ge(x_ready, xr + n + 1)
                    squares(x, norm, n)

            ffn_up(U_GU1, N_F1, B_H1, None, None, 0)
            ffn_down(U_DN1, N_MIX, B_H1, B_MIXN, V_MIX, 0)

            fill(5)
            take(B_MIXN + 3, 0, xT_hi, 12, V_MIX + 12)
            root(N_MIX)
            fill(4 * U_G - 5)

            act.wait_ge(z_ready, 4)
            for t in range(NT):
                last = nc.scalar.activation(gate[:, t], z_n[:, t, C_GATE:].rearrange("p (h b) -> p h b", b=3),
                                            ACT.Sigmoid)
            last.then_inc(gates_ready, 1)
            fill(8 * FILL_ROPE + FILL_ROPED)
            for b in range(2):
                act.wait_ge(q_turned, b + 1)
                nc.scalar.activation(qT[:, 4 * b:4 * b + 4, :], turn[b], ACT.Copy).then_inc(q_taken, 1)
            fill(FILL_Q)
            act.wait_ge(k_turned, 1)
            nc.scalar.activation(kT[:].rearrange("p b g s -> p (b g) s"), turn[0], ACT.Copy).then_inc(k_taken, 1)
            act.wait_ge(blk_ready, 1)
            nc.scalar.activation(blk_hi[:], blk[:], ACT.Copy).then_inc(blk_hi_ready, 1)
            fill(FILL_K)
            fill(FILL_CMP)
            act.wait_ge(unit_done, U_CMP + U_G)
            nc.scalar.activation(hid[0:32, :], psum[0:32, 0, 0:CMP_HIDDEN], ACT.Silu)
            nc.scalar.activation(hid[32:64, :], psum[32:64, 0, CMP_HIDDEN:2 * CMP_HIDDEN], ACT.Silu)\
              .then_inc(hid_ready, 1)
            fill(FILL_HID)
            fill(FILL_KV)
            fill(FILL_SC)
            for t in range(NT):
                act.wait_ge(sc_ready, t + 1)
                nc.scalar.activation(pc[:, t, :], pc[:, t, :], ACT.Exp, scale=DH ** -0.5).then_inc(ec_ready, 1)
            fill(FILL_PC)
            act.wait_ge(pc_turned, 1)
            nc.scalar.activation(pcT[0:REP * N_CMP], psum[0:REP * N_CMP, 6, :].rearrange("p (t g s) -> p t g s", t=NT, g=2),
                                 ACT.Copy).then_inc(pcT_ready, 1)

            def width(i):
                return P if i < 8 else 2 * P

            def exps(i):
                t, h0 = i // 8, 2 * (i % 8)
                act.wait_ge(s_taken, i + 1)
                for hh in range(2):
                    for b in range(2):
                        w = width(i)
                        r = prob[i % 3][:, hh, b * w:(b + 1) * w]
                        last = nc.scalar.activation(r, r, ACT.Exp, scale=DH ** -0.5,
                                                    bias=mx[:, t, h0 + hh, b:b + 1],
                                                    accum_out=sm[:, t, h0 + hh, b:b + 1])
                last.then_inc(e_ready, 1)

            def takeT(m):
                act.wait_ge(p_turned, m + 1)
                if m >= 2:
                    act.wait_ge(pv_done, m - 1)
                w = 2 * width(m // 2)
                nc.scalar.activation(probT[:, m % 2, 0:w], psum[:, 6, 0:w], ACT.Copy).then_inc(pT_ready, 1)

            hg_at = [0]

            def recurrence_step():
                k = hg_at[0]
                hg_at[0] += 1
                if k == 0:
                    for b in range(2):
                        act.wait_ge(f_turned, b + 1)
                        nc.scalar.activation(fT[:, 4 * b:4 * b + 4, :], hturn[b], ACT.Sigmoid).then_inc(f_sig, 1)
                elif k == 1:
                    for b in range(2):
                        act.wait_ge(hq_turned, b + 1)
                        nc.scalar.activation(qfT[:, 4 * b:4 * b + 4, :], hturn[b], ACT.Copy).then_inc(hq_taken, 1)
                elif k == 2:
                    act.wait_ge(z_ready, len(IN_GROUPS))
                    for t in range(NT):
                        last = nc.scalar.activation(z_ig[:, t, HG_W:], z_ig[:, t, HG_W:], ACT.Silu)
                    last.then_inc(g_silu, 1)

            def slot(q):
                if q < SLOTS_U:
                    fill(ITEM_UNITS[q])
                elif hg_at[0] < HG_STEPS:
                    recurrence_step()

            for i in range(18):
                slot(2 * i)
                if i >= 2:
                    takeT(2 * i - 4)
                if i < 16:
                    exps(i)
                slot(2 * i + 1)
                if i >= 2:
                    takeT(2 * i - 3)

            while hg_at[0] < HG_STEPS:
                recurrence_step()
            act.wait_ge(cross_done, 1)
            nc.scalar.activation(att_x[:].rearrange("p h s -> p (h s)"),
                                 psum[:, 0:2, :].rearrange("p b n -> p (b n)"), ACT.Copy).then_inc(cross_taken, 1)
            take(B_MIX, 0, ffT_hi, MIX_HI + 12)
            for t in range(NT):
                act.wait_ge(ho_done, t + 1)
                nc.scalar.activation(fT[:, 4 * t:4 * t + 4, :].rearrange("p h s -> p (h s)"),
                                     psum[:, 2 * t:2 * t + 2, :].rearrange("p b n -> p (b n)"),
                                     ACT.Square).then_inc(ho_sq, 1)
            act.wait_ge(ho_var, 1)
            nc.scalar.activation(hst[:, 2], hst[:, 1], ACT.Sqrt).then_inc(ho_std, 1)
            take(B_MIX + 1, 1, ffT_hi, MIX_HI + 8)

            for n in range(D_CHUNKS):
                for j in range(U_G):
                    step(U_OUT + U_G * n + j)
                    if j == 2 and n == 0:
                        for m in range(2):
                            take(B_MIX + 2 + m, m, ffT_hi, MIX_HI + 4 * m, V_HG + 4 * m)
                    if j == 4 and n:
                        take(B_XAN + n - 1, 0, xT_hi, 4 * (n - 1), V_XA + 4 * (n - 1))
                act.wait_ge(x_ready, 4 + n + 1)
                squares(x, N_XA, n)
            for j in range(U_G):
                step(U_XQ + j)
                if j == 4:
                    take(B_XAN + 3, 0, xT_hi, 12, V_XA + 12)
                    root(N_XA)
            act.wait_ge(qx_turned, 1)
            nc.scalar.activation(qxT[:], turn[0], ACT.Copy).then_inc(qx_taken, 1)
            for h in range(X_HEADS):
                act.wait_ge(xm_ready, h + 1)
                for t in range(NT):
                    last = nc.scalar.activation(px[:, h, t, :], psum[:, 4 + h, t * MEM:(t + 1) * MEM], ACT.Exp,
                                                scale=X_DH ** -0.5, bias=xst[:, 0, h, t:t + 1],
                                                accum_out=xst[:, 1, h, t:t + 1])
                last.then_inc(xe_ready, 1)
            for h in range(X_HEADS):
                act.wait_ge(xp_turned, h + 1)
                nc.scalar.activation(pxT[:, h].rearrange("p k s -> p (k s)"), psum[:, 4 + h, :], ACT.Copy)\
                  .then_inc(xpT_ready, 1)
            act.wait_ge(xo_done, 1)
            nc.scalar.activation(ffT_hi[:, OX:OX + 4, :], turn[0], ACT.Copy).then_inc(xo_hi, 1)
            for n in range(D_CHUNKS):
                for j in range(U_XOG):
                    step(U_XO + U_XOG * n + j)
                act.wait_ge(x_ready, 8 + n + 1)
                squares(x, N_F2, n)
                if n:
                    take(B_F2N + n - 1, 0, xT_hi, 4 * (n - 1), V_F2 + 4 * (n - 1))

            ffn_up(U_GU2, N_F2, B_H2, B_F2N + 3, V_F2, FF_CHUNKS)
            ffn_down(U_DN2, N_FIN, B_H2, None, None, 12)
            root(N_FIN)
            act.wait_ge(fn_applied, NT)
            act.wait_ge(rstd_ready, N_FIN + 1)
            nc.scalar.activation(x[:, 1, 0:D - NW], x[:, 1, 0:D - NW], ACT.Copy, scale=rstd[:, N_FIN, 1:2])\
              .then_inc(out_scaled, 1)

        @block.vector
        def _(dve):
            chain = [0]

            def link(ins):
                chain[0] += 1
                ins.then_inc(dve_step, 1)
                dve.wait_ge(dve_step, chain[0])

            def split(u, slot):
                dve.wait_ge(w_hi_ready, u + 1)
                nc.vector.tensor_tensor(w_lo[:, slot], w_raw[:, slot], w_hi[:, slot].bitcast(F32), ALU.subtract)\
                  .then_inc(w_lo_ready, 1)

            def step(u):
                if u + SLOTS < U_END:
                    split(u + SLOTS, u % SLOTS)

            mid = [0]

            def fill(n):
                for _ in range(n):
                    g, j = MID[mid[0]]
                    u = U_IN + mid[0]
                    step(u)
                    mid[0] += 1
                    if g != CMP and j == U_G - 1:
                        c0, width = IN_GROUPS[g]
                        dst, d0 = ((z_n, c0 - C_NSA) if c0 >= C_NSA else
                                   (z_ig, c0 - 2 * HG_W) if c0 >= 2 * HG_W else (z_qf, c0))
                        dve.wait_ge(unit_done, u + 1)
                        for t in range(NT):
                            last = nc.vector.tensor_scalar(dst[:, t, d0:d0 + width], pair[g % 2][:, t, 0:width],
                                                           rstd[:, N_MIX, t:t + 1], None, ALU.mult)
                        last.then_inc(z_ready, 1)

            def take(b, pos, lo, klo, hi, khi, scale=None):
                dve.wait_ge(turn_hi, b + 1)
                if scale is None:
                    dyn = not isinstance(klo, int)
                    lo_v = lo[:, bass.ts(klo[0], 4), :] if dyn else lo[:, klo:klo + 4, :]
                    hi_v = hi[:, bass.ts(khi[0], 4), :] if dyn else hi[:, khi:khi + 4, :]
                    nc.vector.tensor_tensor(lo_v, turn[pos], hi_v.bitcast(F32), ALU.subtract).then_inc(turn_lo, 1)
                    return
                for j in range(4):
                    last = nc.vector.scalar_tensor_tensor(
                        out=lo[:, klo + j, :], in0=turn[pos][:, j, :], scalar=vec[:, scale + j:scale + j + 1],
                        in1=hi[:, khi + j, :].bitcast(F32), op0=ALU.mult, op1=ALU.subtract)
                last.then_inc(turn_lo, 1)

            def variance(norm, sq):
                dve.wait_ge(sq_done, sq)
                link(nc.vector.tensor_reduce(var[:, norm, :], ss[:, norm], AX_X, ALU.add))
                nc.vector.tensor_scalar(var[:, norm, :], var[:, norm, :], 1.0 / D, EPS, ALU.mult, ALU.add)\
                  .then_inc(var_ready, 1)

            def inverse(norm):
                dve.wait_ge(std_ready, norm + 1)
                nc.vector.reciprocal(rstd[:, norm, :], std[:, norm, :]).then_inc(rstd_ready, 1)
                dve.wait_ge(rstd_ready, norm + 1)

            dve.wait_ge(vec_turned, 1)
            nc.vector.tensor_copy(vec[:], psum[:, 7, 0:V_ROWS]).then_inc(vec_ready, 1)
            for n in range(4):
                take(B_MEM + n, n % 2, ffT_lo, MEM_T + 4 * n, ffT_hi, MEM_T + 4 * n, V_MEM + 4 * n)
                split(n, n)
            variance(N_MEM, 4)
            dve.wait_ge(vec_ready, 1)
            l0, l1 = vec[:, V_LB:V_LB + 8], vec[:, V_LB + 8:V_LB + 16]
            link(nc.vector.tensor_tensor(lb_w[:, 4, :], l0, l1, ALU.max))
            nc.vector.tensor_tensor(lb_w[:, 0, :], l0, lb_w[:, 4, :], ALU.subtract)
            nc.vector.tensor_tensor(lb_w[:, 1, :], l1, lb_w[:, 4, :], ALU.subtract).then_inc(lb_exp, 1)
            inverse(N_MEM)
            dve.wait_ge(lb_exp, 2)
            link(nc.vector.tensor_tensor(lb_w[:, 4, :], lb_w[:, 2, :], lb_w[:, 3, :], ALU.add))
            link(nc.vector.reciprocal(lb_w[:, 4, :], lb_w[:, 4, :]))
            link(nc.vector.tensor_tensor(lb_w[:, 0, :], lb_w[:, 2, :], lb_w[:, 4, :], ALU.mult))
            link(nc.vector.tensor_scalar(lb_w[:, 1, :], lb_w[:, 0, :], -1.0, 1.0, ALU.mult, ALU.add))
            dve.wait_ge(const_loaded, 16 * 8)
            link(nc.vector.tensor_copy(pos_f[:], pos_i[:]))
            for t in range(NT):
                last = nc.vector.tensor_scalar(ang[:, 0, t, :], inv_f[:], pos_f[:, t:t + 1], None, ALU.mult)
            link(last)
            a0, a1, a2, a3 = (ang[:, i] for i in range(4))
            link(nc.vector.tensor_scalar(a3, a0, 1.0 / TWO_PI, ROUND, ALU.mult, ALU.add))
            link(nc.vector.tensor_scalar(a3, a3, -ROUND, None, ALU.add))
            for part, (src, dst) in zip((PI_A, PI_B, PI_C), ((a0, a1), (a1, a2), (a2, a1))):
                link(nc.vector.scalar_tensor_tensor(out=dst, in0=a3, scalar=-part, in1=src,
                                                    op0=ALU.mult, op1=ALU.add))
            link(nc.vector.tensor_scalar(a1, a1, 3.14159, -3.14159, ALU.min, ALU.max))
            link(nc.vector.scalar_tensor_tensor(out=a2, in0=a1, scalar=-1.0, in1=a1, op0=ALU.mult, op1=ALU.min))
            nc.vector.tensor_scalar(a2, a2, TWO_PI / 4, None, ALU.add).then_inc(trig_args, 1)
            for j in range(U_G):
                step(U_MEMK + j)
                if j % 2 == 1:
                    n = j // 2
                    take(B_X + n, n % 2, xT_lo, 4 * n, xT_hi, 4 * n, V_F1 + 4 * n)
            dve.wait_ge(unit_done, U_MEMK + U_G)
            for t in range(NT):
                last = nc.vector.tensor_scalar(hb[:, t, :], pair[0][:, t, :], rstd[:, N_MEM, t:t + 1], None, ALU.mult)
            last.then_inc(kv_taken, 1)
            for j in range(U_G):
                step(U_MEMV + j)
                if j == 2:
                    dve.wait_ge(turn_hi, B_KX + 1)
                    nc.vector.tensor_copy(kxT[:, 2:4, :], turn[0][:, 2:4, :]).then_inc(turn_lo, 1)
            variance(N_F1, 8)
            dve.wait_ge(unit_done, U_MEMV + U_G)
            for t in range(NT):
                last = nc.vector.tensor_scalar(vx[:, t, :], pair[1][:, t, :], rstd[:, N_MEM, t:t + 1], None, ALU.mult)
            last.then_inc(kv_taken, 1)
            inverse(N_F1)

            def ffn_up(u0, norm, b_h, b_x3, s_x3, base_c, sq):
                def body(ch, first):
                    for k in range(2 * U_G):
                        u = u0 + 2 * U_G * ch + k
                        split(u + SLOTS, (u0 + k) % SLOTS)
                        if k == 4:
                            if not first:
                                take(b_h - 1 + ch, 0, ffT_lo, (ch - 1,), ffT_hi, (ch - 1,))
                            elif b_x3 is not None:
                                take(b_x3, 0, xT_lo, 12, xT_hi, 12, s_x3 + 12)
                                variance(norm, sq)
                                inverse(norm)
                    dve.wait_ge(unit_done, u + 1)
                    dve.wait_ge(gate_ready, base_c + 1 + ch)
                    dve.wait_ge(turned, b_h + ch)
                    for t in range(NT):
                        last = nc.vector.scalar_tensor_tensor(
                            out=hb[:, t, :], in0=pair[1][:, t, :], scalar=rstd[:, norm, t:t + 1],
                            in1=sg[:, t, :], op0=ALU.mult, op1=ALU.mult)
                    last.then_inc(h_ready, 1)

                body(0, True)
                with dve.Fori(1, FF_CHUNKS) as ch:
                    body(ch, False)

            def residual(src, n, factor):
                for t in range(NT):
                    xc = x[:, t, n * NW:(n + 1) * NW]
                    last = nc.vector.scalar_tensor_tensor(out=xc, in0=src[:, t, :], scalar=factor, in1=xc,
                                                          op0=ALU.mult, op1=ALU.add)
                last.then_inc(x_ready, 1)

            def ffn_down(u0, b_h, b_x, s_x):
                for n in range(D_CHUNKS):
                    for k in range(U_D):
                        step(u0 + U_D * n + k)
                        if k == 4:
                            if n == 0:
                                take(b_h + FF_CHUNKS - 1, 0, ffT_lo, KF - 4, ffT_hi, KF - 4)
                            elif b_x is not None:
                                take(b_x + n - 1, 0, xT_lo, 4 * (n - 1), xT_hi, 4 * (n - 1), s_x + 4 * (n - 1))
                    if b_x is None and n == D_CHUNKS - 1:
                        dve.wait_ge(sq_done, 24 - 1)
                        dve.wait_ge(fn_loaded, 16)
                        for t in range(NT):
                            nc.vector.tensor_tensor(x[:, t, 0:D - NW], x[:, t, 0:D - NW], fnorm[:, 0:D - NW], ALU.mult)\
                              .then_inc(fn_applied, 1)
                    dve.wait_ge(unit_done, u0 + U_D * (n + 1))
                    residual(pair[n % 2], n, 0.5)

            ffn_up(U_GU1, N_F1, B_H1, None, None, 0, 8)
            ffn_down(U_DN1, B_H1, B_MIXN, V_MIX)

            fill(5)
            take(B_MIXN + 3, 0, xT_lo, 12, xT_hi, 12, V_MIX + 12)
            variance(N_MIX, 12)
            inverse(N_MIX)
            fill(4 * U_G - 5)
            dve.wait_ge(z_ready, 4)

            dve.wait_ge(trig_ready, 1)
            for t in range(NT):
                qv = z_n[:, t, 0:C_KV].rearrange("p (h x d) -> p h x d", x=2, d=DH // 2)
                kv = z_n[:, t, C_KV:C_GATE].rearrange("p (a b g x d) -> p a b g x d", a=3, b=2, g=2, x=2)
                for part in range(4):
                    v, n = (qv, NSA_HEADS) if part == 0 else (kv[:, part - 1, 0], NSA_KV)
                    t1, t2 = v[:, :, 0, :], v[:, :, 1, :]
                    tmp = [rtmp[:, i, 0:n * DH // 2].rearrange("p (h d) -> p h d", d=DH // 2) for i in range(4)]
                    cosb = cos_t[:, t, :].unsqueeze(1).broadcast_to([P, n, DH // 2])
                    sinb = sin_t[:, t, :].unsqueeze(1).broadcast_to([P, n, DH // 2])
                    nc.vector.tensor_tensor(tmp[0], t1, cosb, ALU.mult)
                    nc.vector.tensor_tensor(tmp[1], t2, sinb, ALU.mult)
                    nc.vector.tensor_tensor(tmp[2], t2, cosb, ALU.mult)
                    link(nc.vector.tensor_tensor(tmp[3], t1, sinb, ALU.mult))
                    nc.vector.tensor_tensor(t1, tmp[0], tmp[1], ALU.subtract)
                    link(nc.vector.tensor_tensor(t2, tmp[2], tmp[3], ALU.add))
                    if t == NT - 1 and part == 3:
                        nc.vector.memset(blk[:], 0.0).then_inc(roped, 1)
                    fill(FILL_ROPE)
            dve.wait_ge(roped, 1)
            fill(FILL_ROPED + FILL_Q)
            dve.wait_ge(tok_turned, 1)
            pe_t = vec[:, V_PE:V_PE + 16]
            for xg in range(4):
                for e in range(2):
                    last = nc.vector.tensor_tensor(
                        blk[:, 8 * e:8 * e + 8, xg * CPAD:xg * CPAD + N_CMP],
                        psum[:, 6, xg * P + 8 * e:xg * P + 8 * e + 8 * N_CMP].rearrange("p (n b) -> p b n", b=8),
                        pe_t[:, 8 * e:8 * e + 8].unsqueeze(2).broadcast_to([P, 8, N_CMP]), ALU.add)
            last.then_inc(blk_ready, 1)
            dve.wait_ge(blk_hi_ready, 1)
            nc.vector.tensor_tensor(blk_lo[:], blk[:], blk_hi[:].bitcast(F32), ALU.subtract).then_inc(blk_lo_ready, 1)
            fill(FILL_K)
            fill(FILL_CMP)
            fill(FILL_HID)
            dve.wait_ge(hid_turned, 1)
            hid_ps = psum[:, 4, 0:128].rearrange("p (k r) -> p k r", k=2)
            nc.vector.tensor_copy(hidT[:], hid_ps)
            for k in range(2):
                for g in range(NSA_KV):
                    last = nc.vector.tensor_copy(
                        hid_rep[:, k, g, :].rearrange("p (r n) -> p r n", n=N_CMP),
                        hid_ps[:, k, 32 + g * CPAD:32 + g * CPAD + N_CMP].unsqueeze(1).broadcast_to([P, REP, N_CMP]))
            last.then_inc(hidT_ready, 1)
            fill(FILL_KV)
            dve.wait_ge(kvc_done, 1)
            nc.vector.tensor_copy(kcT[:], psum[:, 5, 0:32])
            n_rows = REP * N_CMP
            for g in range(NSA_KV):
                last = nc.vector.tensor_tensor(
                    v_blk[0:n_rows, g, :].rearrange("p (r d) -> p r d", d=DH),
                    psum[0:n_rows, 5, 64 + g * DH:64 + (g + 1) * DH].unsqueeze(1).broadcast_to([n_rows, REP, DH]),
                    diag_blk[0:n_rows, :].unsqueeze(2).broadcast_to([n_rows, REP, DH]), ALU.mult)
            last.then_inc(kvc_ready, 1)
            dve.wait_ge(gates_ready, 1)
            fill(FILL_SC)
            for t in range(NT):
                p3 = pc[:, t, :].rearrange("p (h n) -> p h n", n=N_CMP)
                sh = [P, NSA_HEADS, N_CMP]
                cm, cs = cstat[:, t, 0, :], cstat[:, t, 1, :]
                dve.wait_ge(sc_done, NT)
                link(nc.vector.tensor_tensor(
                    pc[:, t, :].rearrange("p (j e n) -> p e j n", e=2, n=N_CMP),
                    psum[:, 6:8, t * REP * N_CMP:(t + 1) * REP * N_CMP].rearrange("p e (j n) -> p e j n", n=N_CMP),
                    cmp_add[:, t, :].unsqueeze(1).unsqueeze(1).broadcast_to([P, 2, REP, N_CMP]), ALU.add))
                link(nc.vector.tensor_reduce(cm, p3, AX_X, ALU.max))
                nc.vector.tensor_tensor(p3, p3, cm.unsqueeze(2).broadcast_to(sh), ALU.subtract).then_inc(sc_ready, 1)
            for t in range(NT):
                p3 = pc[:, t, :].rearrange("p (h n) -> p h n", n=N_CMP)
                cm, cs = cstat[:, t, 0, :], cstat[:, t, 1, :]
                dve.wait_ge(ec_ready, t + 1)
                link(nc.vector.tensor_tensor(p3, p3, cmp_mul[:, t, :].unsqueeze(1).broadcast_to(sh), ALU.mult))
                link(nc.vector.tensor_reduce(cs, p3, AX_X, ALU.add))
                link(nc.vector.tensor_scalar(cs, cs, 1e-30, None, ALU.max))
                link(nc.vector.reciprocal(cs, cs))
                link(nc.vector.tensor_tensor(cs, cs, gate[:, t, :, 0], ALU.mult))
                nc.vector.tensor_tensor(p3, p3, cs.unsqueeze(2).broadcast_to(sh), ALU.mult).then_inc(pc_ready, 1)
            fill(FILL_PC)

            def maxima(i):
                t, h0 = i // 8, 2 * (i % 8)
                w = P if t == 0 else 2 * P
                dve.wait_ge(s_done, i + 1)
                if i >= 3:
                    dve.wait_ge(p_turned, 2 * (i - 2))
                for hh in range(2):
                    for b in range(2):
                        last = nc.vector.tensor_tensor_reduce(
                            out=prob[i % 3][:, hh, b * w:(b + 1) * w], in0=psum[:, 4 + hh, b * w:(b + 1) * w],
                            in1=causal[:, SEQ - w:SEQ], scale=1.0, scalar=-3e38, op0=ALU.add, op1=ALU.max,
                            accum_out=mx[:, t, h0 + hh, b:b + 1])
                link(last)
                nc.vector.tensor_scalar(mx[:, t, h0:h0 + 2, :], mx[:, t, h0:h0 + 2, :], -DH ** -0.5, None, ALU.mult)\
                  .then_inc(s_taken, 1)

            def weigh(i):
                t, h0 = i // 8, 2 * (i % 8)
                w = P if t == 0 else 2 * P
                r = rc[:, t, h0:h0 + 2, :]
                dve.wait_ge(e_ready, i + 1)
                link(nc.vector.tensor_scalar(r, sm[:, t, h0:h0 + 2, :], 1e-30, None, ALU.max))
                link(nc.vector.reciprocal(r, r))
                link(nc.vector.tensor_tensor(r, r, gate[:, t, h0:h0 + 2, 1:3], ALU.mult))
                for hh in range(2):
                    for b in range(2):
                        p = prob[i % 3][:, hh, b * w:(b + 1) * w]
                        last = nc.vector.tensor_scalar(p, p, rc[:, t, h0 + hh, b:b + 1], None, ALU.mult)
                last.then_inc(p_ready, 1)

            def take_o(k):
                t, g = k // 2, k % 2
                dve.wait_ge(pv_done, REP * (k + 1))
                nc.vector.tensor_copy(z_n[:, t, g * 512:(g + 1) * 512], psum[:, 7, :]).then_inc(o_taken, 1)

            hg_at = [0]

            def recurrence_step():
                k = hg_at[0]
                hg_at[0] += 1
                if k == 0:
                    return
                if k == 1:
                    dve.wait_ge(f_sig, 2)
                    for h in range(HG_HEADS):
                        last = nc.vector.tensor_scalar(fT[:, h, :], fT[:, h, :], lb_w[:, 1, h:h + 1],
                                                       lb_w[:, 0, h:h + 1], ALU.mult, ALU.add)
                    link(last)
                    nc.vector.tensor_scalar(kgT[:], fT[:], -1.0, 1.0, ALU.mult, ALU.add).then_inc(kf_ready, 1)
                    return
                if k == 2:
                    for b in range(4):
                        dve.wait_ge(dg_done, b + 1)
                        nc.vector.tensor_tensor(att[:, 2 * b:2 * b + 2].rearrange("p h t s -> p (h t) s"),
                                                psum[:, b, :].rearrange("p (c s) -> p c s", s=P),
                                                ident[:].unsqueeze(1).broadcast_to([P, 4, P]), ALU.mult)\
                          .then_inc(dg_taken, 1)
                    for half in range(2):
                        hs = slice(4 * half, 4 * half + 4)
                        nc.vector.tensor_tensor(qfT[:, hs], qfT[:, hs], fT[:, hs], ALU.mult).then_inc(qk_ready, 1)
                    dve.wait_ge(mask_loaded, 16)
                    link(nc.vector.tensor_copy(lvl_mask[:], lvl_f32[:]))
                    return
                n = k - 3
                l, half = n // 2, n % 2
                m = LEVELS[l]
                hs = slice(4 * half, 4 * half + 4)
                dve.wait_ge(qk_ready, n + 1)
                dve.wait_ge(lv_done, n + 1)
                q4 = qfT[:, hs].rearrange("p h (b x m) -> p (h b) x m", x=2, m=m)
                k4 = kgT[:, hs].rearrange("p h (b x m) -> p (h b) x m", x=2, m=m)
                t4 = tots[m][:, hs].rearrange("p h (b x) -> p (h b) x", x=2)
                nb = HG_HEADS // 2 * SEQ // (2 * m)
                if m < LEVELS[-1]:
                    nc.vector.tensor_tensor(tots[2 * m][:, hs].rearrange("p h b -> p (h b)"),
                                            t4[:, :, 0], t4[:, :, 1], ALU.mult)
                nc.vector.tensor_tensor(q4[:, :, 1, :], q4[:, :, 1, :],
                                        t4[:, :, 0].unsqueeze(2).broadcast_to([P, nb, m]), ALU.mult)
                nc.vector.tensor_tensor(k4[:, :, 0, :], k4[:, :, 0, :],
                                        t4[:, :, 1].unsqueeze(2).broadcast_to([P, nb, m]),
                                        ALU.mult).then_inc(qk_ready, 1)
                if l:
                    dve.wait_ge(lv_taken, n - 1)
                a5 = att[:, hs].rearrange("p h t (b x m) -> p (h t) b x m", x=2, m=m)
                m4 = lvl_mask[:, l, :].rearrange("p (b m) -> p b m", m=m).unsqueeze(1)
                nc.vector.copy_predicated(
                    a5[:, :, :, 1, :], m4.broadcast_to([P, 8, P // (2 * m), m]),
                    psum[:, n % 4, :].rearrange("p (c b m) -> p c b m", c=8, m=m)).then_inc(lv_taken, 1)

            def slot(q):
                if q < SLOTS_U:
                    fill(ITEM_UNITS[q])
                elif hg_at[0] < HG_STEPS:
                    recurrence_step()

            for i in range(18):
                if i < 16:
                    maxima(i)
                slot(2 * i)
                if i >= 6 and i % 4 == 2 and i < 18:
                    take_o(i // 4 - 1)
                if 1 <= i < 17:
                    weigh(i - 1)
                slot(2 * i + 1)
            take_o(3)

            while hg_at[0] < HG_STEPS:
                recurrence_step()
            take(B_MIX, 0, ffT_lo, MIX_LO + 12, ffT_hi, MIX_HI + 12)
            dve.wait_ge(g_silu, 1)
            for t in range(NT):
                dve.wait_ge(ho_sq, t + 1)
                nc.vector.tensor_tensor(z_ig[:, t, HG_W:], z_ig[:, t, HG_W:],
                                        psum[:, 2 * t:2 * t + 2, :].rearrange("p b n -> p (b n)"), ALU.mult)\
                  .then_inc(ho_gated, 1)
                last = nc.vector.tensor_reduce(hst[:, 0, t, :], fT[:, 4 * t:4 * t + 4, :].rearrange("p h (x d) -> p (h x) d", x=2),
                                               AX_X, ALU.add)
            link(last)
            nc.vector.tensor_scalar(hst[:, 1], hst[:, 0], 1.0 / HG_D, EPS, ALU.mult, ALU.add).then_inc(ho_var, 1)
            take(B_MIX + 1, 1, ffT_lo, MIX_LO + 8, ffT_hi, MIX_HI + 8)
            dve.wait_ge(ho_std, 1)
            link(nc.vector.reciprocal(hst[:, 3], hst[:, 2]))
            dve.wait_ge(ho_gated, NT)
            for t in range(NT):
                o3v = z_ig[:, t, HG_W:].rearrange("p (h d) -> p h d", d=HG_D)
                last = nc.vector.tensor_tensor(o3v, o3v, hst[:, 3, t, :].unsqueeze(2).broadcast_to([P, HG_HEADS, HG_D]),
                                               ALU.mult)
            last.then_inc(mix_ready, 1)

            for n in range(D_CHUNKS):
                for j in range(U_G):
                    step(U_OUT + U_G * n + j)
                    if j == 2 and n == 0:
                        for m in range(2):
                            take(B_MIX + 2 + m, m, ffT_lo, MIX_LO + 4 * m, ffT_hi, MIX_HI + 4 * m, V_HG + 4 * m)
                    if j == 4 and n:
                        take(B_XAN + n - 1, 0, xT_lo, 4 * (n - 1), xT_hi, 4 * (n - 1), V_XA + 4 * (n - 1))
                dve.wait_ge(unit_done, U_OUT + U_G * (n + 1))
                residual(pair[n % 2], n, 1.0)
            for j in range(U_G):
                step(U_XQ + j)
                if j == 4:
                    take(B_XAN + 3, 0, xT_lo, 12, xT_hi, 12, V_XA + 12)
                    variance(N_XA, 16)
                    inverse(N_XA)
            dve.wait_ge(unit_done, U_XQ + U_G)
            for t in range(NT):
                last = nc.vector.tensor_scalar(qx[:, t, :], pair[0][:, t, :], rstd[:, N_XA, t:t + 1], None, ALU.mult)
            last.then_inc(qx_ready, 1)
            for h in range(X_HEADS):
                dve.wait_ge(xs_done, h + 1)
                link(nc.vector.tensor_reduce(xst[:, 2, h, :], psum[:, 4 + h, :].rearrange("p (t s) -> p t s", t=NT),
                                             AX_X, ALU.max))
                nc.vector.tensor_scalar(xst[:, 0, h, :], xst[:, 2, h, :], -X_DH ** -0.5, None, ALU.mult)\
                  .then_inc(xm_ready, 1)
            for h in range(X_HEADS):
                dve.wait_ge(xe_ready, h + 1)
                link(nc.vector.reciprocal(xst[:, 2, h, :], xst[:, 1, h, :]))
                for t in range(NT):
                    last = nc.vector.tensor_scalar(px[:, h, t, :], px[:, h, t, :], xst[:, 2, h, t:t + 1], None, ALU.mult)
                last.then_inc(xp_ready, 1)
            dve.wait_ge(xo_hi, 1)
            nc.vector.tensor_tensor(ffT_lo[:, OX:OX + 4, :], turn[0], ffT_hi[:, OX:OX + 4, :].bitcast(F32),
                                    ALU.subtract).then_inc(xo_lo, 1)
            for n in range(D_CHUNKS):
                for j in range(U_XOG):
                    step(U_XO + U_XOG * n + j)
                dve.wait_ge(unit_done, U_XO + U_XOG * (n + 1))
                residual(pair[(n + 1) % 2], n, 1.0)
                if n:
                    take(B_F2N + n - 1, 0, xT_lo, 4 * (n - 1), xT_hi, 4 * (n - 1), V_F2 + 4 * (n - 1))

            ffn_up(U_GU2, N_F2, B_H2, B_F2N + 3, V_F2, FF_CHUNKS, 20)
            ffn_down(U_DN2, B_H2, None, None)
            variance(N_FIN, 24)
            inverse(N_FIN)
            nc.vector.tensor_scalar(x[:, 0, 0:D - NW], x[:, 0, 0:D - NW], rstd[:, N_FIN, 0:1], None, ALU.mult)\
              .then_inc(out_ready, 1)
            for t in range(NT):
                nc.vector.scalar_tensor_tensor(out=x[:, t, D - NW:], in0=x[:, t, D - NW:], scalar=rstd[:, N_FIN, t:t + 1],
                                               in1=fnorm[:, D - NW:], op0=ALU.mult, op1=ALU.mult).then_inc(out_ready, 1)

        @block.tensor
        def _(pe):
            def unit(u, slot, hi, khi, lo, klo, dst, width, first, last):
                pe.wait_ge(w_lo_ready, u + 1)
                for kk in range(KT_U):
                    for t in range(NT):
                        ts = slice(t * P, (t + 1) * P)
                        passes = ((hi[:, khi + kk, ts], w_hi), (hi[:, khi + kk, ts], w_lo), (lo[:, klo + kk, ts], w_hi))
                        for n, (act_t, w) in enumerate(passes):
                            mm = nc.tensor.matmul(dst[:, t, 0:width], act_t, w[:, slot, kk, 0:width],
                                                  start=(first and kk == 0 and n == 0),
                                                  stop=(last and kk == KT_U - 1 and n == 2))
                mm.then_inc(unit_done, 1)

            def batch(b, pos, src, wait_taken=True):
                if wait_taken:
                    pe.wait_ge(turn_lo, b)
                for j in range(4):
                    for t in range(NT):
                        tr = nc.tensor.transpose(turn[pos][:, j, t * P:(t + 1) * P], src(j, t), ident[:])
                tr.then_inc(turned, 1)

            def x_tiles(n):
                return lambda j, t: x[:, t, (4 * n + j) * P:(4 * n + j + 1) * P]

            pe.wait_ge(vec_loaded, 16 * 9)
            nc.tensor.transpose(psum[:, 7, 0:V_ROWS], vec_rows[0:V_ROWS, :], ident[0:V_ROWS, 0:V_ROWS])\
              .then_inc(vec_turned, 1)
            for n in range(4):
                pe.wait_ge(mem_loaded[n], 16)
                if n == 1:
                    pe.wait_ge(vec_ready, 1)
                if n >= 2:
                    pe.wait_ge(turn_lo, B_MEM + n - 1)
                batch(B_MEM + n, n % 2, lambda j, t: mem_x[:, t, (4 * n + j) * P:(4 * n + j + 1) * P], False)
            for g, u0 in enumerate((U_MEMK, U_MEMV)):
                for j in range(U_G):
                    if g == 0 and j % 2 == 0:
                        pe.wait_ge(turn_lo, B_MEM + j // 2 + 1)
                    unit(u0 + j, (u0 + j) % SLOTS, ffT_hi, MEM_T + 2 * j, ffT_lo, MEM_T + 2 * j, pair[g], NW,
                         j == 0, j == U_G - 1)
                    if g == 0 and j % 2 == 0:
                        n = j // 2
                        pe.wait_ge(x_loaded[n], 16)
                        pe.wait_ge(turn_lo, B_X + n - 1)
                        batch(B_X + n, n % 2, x_tiles(n), False)
                    if g == 1 and j == 1:
                        pe.wait_ge(kv_taken, 1)
                        batch(B_KX, 0, lambda h, t: hb[:, t, h * P:(h + 1) * P])

            def ffn_up(u0, b_x, b_h, b_x3, free_a, free_b, base_c):
                def body(ch, first):
                    for k in range(2 * U_G):
                        g, j = k // U_G, k % U_G
                        if first and g == 0 and j % 2 == 0:
                            pe.wait_ge(turn_lo, b_x + j // 2 + 1)
                        if k == 0:
                            pe.wait_ge(*free_a) if first else pe.wait_ge(gate_ready, base_c + ch)
                        if k == U_G:
                            pe.wait_ge(*free_b) if first else pe.wait_ge(h_ready, base_c + ch)
                        unit(u0 + 2 * U_G * ch + k, (u0 + k) % SLOTS, xT_hi, 2 * j, xT_lo, 2 * j, pair[g], NW,
                             j == 0, j == U_G - 1)
                        if k == 3:
                            if not first:
                                pe.wait_ge(h_ready, base_c + ch)
                                batch(b_h - 1 + ch, 0, lambda j, t: hb[:, t, j * P:(j + 1) * P])
                            elif b_x3 is not None:
                                pe.wait_ge(x_ready, 12)
                                batch(b_x3, 0, x_tiles(3))

                body(0, True)
                with pe.Fori(1, FF_CHUNKS) as ch:
                    body(ch, False)

            def ffn_down(u0, b_h, b_x, base_c, xr):
                for n in range(D_CHUNKS):
                    for k in range(U_D):
                        if n == 0 and k == 0:
                            pe.wait_ge(gate_ready, base_c + FF_CHUNKS)
                        if n == 1 and k == 0:
                            pe.wait_ge(h_ready, base_c + FF_CHUNKS)
                        if n >= 2 and k == 0:
                            pe.wait_ge(x_ready, xr + n - 1)
                        if n == 0 and k == U_D - 2:
                            pe.wait_ge(turn_lo, b_h + FF_CHUNKS)
                        u = u0 + U_D * n + k
                        unit(u, u % SLOTS, ffT_hi, 2 * k, ffT_lo, 2 * k, pair[n % 2], NW, k == 0, k == U_D - 1)
                        if k == 3:
                            if n == 0:
                                pe.wait_ge(h_ready, base_c + FF_CHUNKS)
                                batch(b_h + FF_CHUNKS - 1, 0, lambda j, t: hb[:, t, j * P:(j + 1) * P])
                            elif b_x is not None:
                                pe.wait_ge(x_ready, xr + n)
                                batch(b_x + n - 1, 0, x_tiles(n - 1))

            ffn_up(U_GU1, B_X, B_H1, None, (kv_taken, 1), (kv_taken, 2), 0)
            ffn_down(U_DN1, B_H1, B_MIXN, 0, 0)

            mid = [0]

            def fill(n):
                for _ in range(n):
                    g, j = MID[mid[0]]
                    u = U_IN + mid[0]
                    mid[0] += 1
                    if g == CMP:
                        if j == 0:
                            pe.wait_ge(z_ready, 5)
                        pe.wait_ge(w_lo_ready, u + 1)
                        for kk in range(KT_U):
                            for n_, (tok, w) in enumerate(((blk_hi, w_hi), (blk_hi, w_lo), (blk_lo, w_hi))):
                                mm = nc.tensor.matmul(psum[0:66, 0, :], tok[:, 2 * j + kk, :], w[:, u % SLOTS, kk, :],
                                                      start=(j == 0 and kk == 0 and n_ == 0),
                                                      stop=(j == U_G - 1 and kk == KT_U - 1 and n_ == 2))
                        mm.then_inc(unit_done, 1)
                        continue
                    if j == 0:
                        if g < 2:
                            pe.wait_ge(x_ready, 3 + g)
                        else:
                            pe.wait_ge(z_ready, g - 1)
                        if g == 6:
                            pe.wait_ge(hid_ready, 1)
                    if g == 0 and j % 2 == 0:
                        pe.wait_ge(turn_lo, B_MIXN + j // 2 + 1)
                    unit(u, u % SLOTS, xT_hi, 2 * j, xT_lo, 2 * j, pair[g % 2], IN_GROUPS[g][1],
                         j == 0, j == U_G - 1)

            fill(4)
            pe.wait_ge(x_ready, 4)
            batch(B_MIXN + 3, 0, x_tiles(3))
            fill(4 * U_G - 4)
            fill(8 * FILL_ROPE + FILL_ROPED)

            pe.wait_ge(roped, 1)
            for b in range(2):
                for j in range(4):
                    for t in range(NT):
                        tr = nc.tensor.transpose(turn[b][:, j, t * P:(t + 1) * P],
                                                 z_n[:, t, (4 * b + j) * P:(4 * b + j + 1) * P], ident[:])
                tr.then_inc(q_turned, 1)
            fill(FILL_Q)
            pe.wait_ge(q_taken, 1)
            for b in range(2):
                for g in range(NSA_KV):
                    for t in range(NT):
                        k0 = C_KV + 256 * (b + 1) + g * DH
                        for half in range(2):
                            mm = nc.tensor.matmul(turn[0][half * DH:(half + 1) * DH, 2 * b + g, t * P:(t + 1) * P],
                                                  z_n[:, t, k0:k0 + DH], ident[:], start=True, stop=True)
            mm.then_inc(k_turned, 1)
            pe.wait_ge(q_taken, 2)
            for xk in range(2):
                for g in range(NSA_KV):
                    for t in range(NT):
                        for par in range(2):
                            c0 = (2 * xk + g) * P + t * (P // 2)
                            k0 = C_KV + xk * 128 + g * DH
                            mm = nc.tensor.matmul(psum[par * DH:(par + 1) * DH, 6, c0:c0 + P // 2],
                                                  z_n[:, t, k0:k0 + DH], ident[:, par::2], start=True, stop=True)
            mm.then_inc(tok_turned, 1)
            fill(FILL_K)
            pe.wait_ge(blk_lo_ready, 1)
            fill(FILL_CMP)
            fill(FILL_HID)
            pe.wait_ge(hid_ready, 1)
            pe.wait_ge(k_taken, 1)
            for k in range(2):
                tr = nc.tensor.transpose(psum[:, 4, k * 64:(k + 1) * 64], hid[0:64, k * P:(k + 1) * P], ident[0:64, 0:64])
            tr.then_inc(hid_turned, 1)
            fill(FILL_KV)
            pe.wait_ge(hidT_ready, 1)
            for half in range(2):
                for k in range(2):
                    nc.tensor.matmul(psum[half * DH:(half + 1) * DH, 5, 0:32], w2[:, 0, k, :], hidT[:, k, 0:32],
                                     start=(k == 0), stop=(k == 1))
            for g in range(NSA_KV):
                for k in range(2):
                    mm = nc.tensor.matmul(psum[0:REP * N_CMP, 5, 64 + g * DH:64 + (g + 1) * DH], hid_rep[:, k, g, :],
                                          w2[:, 1, k, :], start=(k == 0), stop=(k == 1))
            mm.then_inc(kvc_done, 1)
            fill(FILL_SC)
            pe.wait_ge(kvc_ready, 1)
            for t in range(NT):
                for h in range(NSA_HEADS):
                    r = slice((h % 2) * DH, (h % 2 + 1) * DH)
                    c0 = (t * REP + h // 2) * N_CMP
                    mm = nc.tensor.matmul(psum[:, 6 + h % 2, c0:c0 + N_CMP], qT[r, h // 2, t * P:(t + 1) * P],
                                          kcT[r, (h // REP) * CPAD:(h // REP) * CPAD + N_CMP], start=True, stop=True)
                mm.then_inc(sc_done, 1)
            fill(FILL_PC)
            for t in range(NT):
                pe.wait_ge(pc_ready, t + 1)
                for g in range(NSA_KV):
                    n_rows = REP * N_CMP
                    tr = nc.tensor.transpose(psum[0:n_rows, 6, (2 * t + g) * P:(2 * t + g + 1) * P],
                                             pc[:, t, g * n_rows:(g + 1) * n_rows], ident[:])
            tr.then_inc(pc_turned, 1)

            def scores(i):
                t, h0 = i // 8, 2 * (i % 8)
                w = P if t == 0 else 2 * P
                if i:
                    pe.wait_ge(s_taken, i)
                for hh in range(2):
                    h = h0 + hh
                    r = slice((h % 2) * DH, (h % 2 + 1) * DH)
                    for b in range(2):
                        mm = nc.tensor.matmul(psum[:, 4 + hh, b * w:(b + 1) * w], qT[r, h // 2, t * P:(t + 1) * P],
                                              kT[r, b, h // REP, 0:w], start=True, stop=True)
                mm.then_inc(s_done, 1)

            def turn_p(m):
                i, hh = m // 2, m % 2
                w = P if i < 8 else 2 * P
                pe.wait_ge(p_ready, i + 1)
                if m == 0:
                    pe.wait_ge(pcT_ready, 1)
                else:
                    pe.wait_ge(pT_ready, m)
                for k in range(2 * w // P):
                    tr = nc.tensor.transpose(psum[:, 6, k * P:(k + 1) * P], prob[i % 3][:, hh, k * P:(k + 1) * P], ident[:])
                tr.then_inc(p_turned, 1)

            def values(m):
                i, hh = m // 2, m % 2
                t, h = i // 8, 2 * (i % 8) + hh
                g, r = h // REP, h % REP
                nk = 1 if t == 0 else 2
                k = 2 * t + g
                pe.wait_ge(pT_ready, m + 1)
                if r == 0:
                    if k:
                        pe.wait_ge(o_taken, k)
                    nc.tensor.matmul(psum[:, 7, :], pcT[0:REP * N_CMP, t, g, :], v_blk[0:REP * N_CMP, g, :],
                                     start=True, stop=False,
                                     skip_group_check=True)
                for b in range(2):
                    for kk in range(nk):
                        c0 = C_KV + 256 * (b + 1) + 128 + g * DH
                        mm = nc.tensor.matmul(psum[:, 7, r * DH:(r + 1) * DH], probT[:, m % 2, (b * nk + kk) * P:(b * nk + kk + 1) * P],
                                              z_n[:, kk, c0:c0 + DH], start=False,
                                              stop=(r == REP - 1 and b == 1 and kk == nk - 1), skip_group_check=True)
                mm.then_inc(pv_done, 1)

            hg_at = [0]

            def recurrence_step():
                k = hg_at[0]
                hg_at[0] += 1
                if k == 0:
                    pe.wait_ge(z_ready, len(IN_GROUPS))
                if k < 2:
                    for b in range(2):
                        if k == 1:
                            pe.wait_ge(f_sig, b + 1)
                        for j in range(4):
                            for t in range(NT):
                                c0 = (HG_W if k == 0 else 0) + (4 * b + j) * HG_D
                                tr = nc.tensor.transpose(hturn[b][:, j, t * P:(t + 1) * P],
                                                         z_qf[:, t, c0:c0 + HG_D], ident[:])
                        tr.then_inc(f_turned if k == 0 else hq_turned, 1)
                    return
                if k == 2:
                    pe.wait_ge(kf_ready, 1)
                    pe.wait_ge(hq_taken, 2)
                    for b in range(4):
                        for hh in range(2):
                            for t in range(NT):
                                h, ts = 2 * b + hh, slice(t * P, (t + 1) * P)
                                mm = nc.tensor.matmul(psum[:, b, (2 * hh + t) * P:(2 * hh + t + 1) * P],
                                                      kgT[:, h, ts], qfT[:, h, ts], start=True, stop=True)
                        mm.then_inc(dg_done, 1)
                    return
                n = k - 3
                half, m = n % 2, LEVELS[n // 2]
                pe.wait_ge(qk_ready, n + 1)
                if n < 4:
                    pe.wait_ge(dg_taken, n + 1)
                else:
                    pe.wait_ge(lv_taken, n - 3)
                for hh in range(4):
                    h = 4 * half + hh
                    for t in range(NT):
                        q_late = qfT[:, h, t * P:(t + 1) * P].rearrange("p (b x m) -> p b x m", x=2, m=m)[:, :, 1, :]
                        c0 = (2 * hh + t) * (P // 2)
                        mm = nc.tensor.matmul(psum[:, n % 4, c0:c0 + P // 2].rearrange("p (b m) -> p b m", m=m),
                                              kgT[:, h, t * P:(t + 1) * P], q_late, start=True, stop=True)
                mm.then_inc(lv_done, 1)

            def slot(q):
                if q < SLOTS_U:
                    fill(ITEM_UNITS[q])
                elif hg_at[0] < HG_STEPS:
                    recurrence_step()

            for i in range(18):
                if i < 16:
                    scores(i)
                slot(2 * i)
                if i >= 2:
                    turn_p(2 * i - 4)
                    if i > 2:
                        values(2 * i - 5)
                slot(2 * i + 1)
                if i >= 2:
                    turn_p(2 * i - 3)
                    values(2 * i - 4)
            values(31)

            while hg_at[0] < HG_STEPS:
                recurrence_step()
            pe.wait_ge(qk_ready, 2 * len(LEVELS) + 2)
            pe.wait_ge(lv_taken, 2 * len(LEVELS))
            for h in range(HG_HEADS):
                mm = nc.tensor.matmul(psum[:, h // 4, (h % 4) * P:(h % 4 + 1) * P], kgT[:, h, 0:P],
                                      qfT[:, h, P:SEQ], start=True, stop=True)
            mm.then_inc(cross_done, 1)
            pe.wait_ge(o_taken, 4)
            batch(B_MIX, 0, lambda j, t: z_n[:, t, (4 + j) * P:(5 + j) * P], False)
            pe.wait_ge(cross_taken, 1)
            for t in range(NT):
                for h in range(HG_HEADS):
                    dst = psum[:, 2 * t + h // 4, (h % 4) * P:(h % 4 + 1) * P]
                    vs = slice(h * HG_D, (h + 1) * HG_D)
                    mm = nc.tensor.matmul(dst, att[:, h, t, :], z_ig[:, t, vs], start=True, stop=(t == 0))
                    if t == 1:
                        mm = nc.tensor.matmul(dst, att_x[:, h, :], z_ig[:, 0, vs], start=False, stop=True)
                mm.then_inc(ho_done, 1)
            batch(B_MIX + 1, 1, lambda j, t: z_n[:, t, j * P:(j + 1) * P], False)
            pe.wait_ge(ho_gated, 1)

            for n in range(D_CHUNKS):
                if n >= 2:
                    pe.wait_ge(x_ready, 4 + n - 1)
                for j in range(U_G):
                    if n == 0 and j % 2 == 0:
                        pe.wait_ge(turn_lo, B_MIX + j // 2 + 1)
                    u = U_OUT + U_G * n + j
                    unit(u, u % SLOTS, ffT_hi, MIX_HI + 2 * OUT_ORDER[j], ffT_lo, MIX_LO + 2 * OUT_ORDER[j],
                         pair[n % 2], NW, j == 0, j == U_G - 1)
                    if j == 2 and n == 0:
                        pe.wait_ge(mix_ready, 1)
                        pe.wait_ge(turn_lo, B_MIX + 2)
                        for m in range(2):
                            batch(B_MIX + 2 + m, m,
                                  lambda j, t: z_ig[:, t, HG_W + (4 * m + j) * P:HG_W + (4 * m + j + 1) * P], False)
                    if j == 3 and n:
                        pe.wait_ge(x_ready, 4 + n)
                        batch(B_XAN + n - 1, 0, x_tiles(n - 1))
            pe.wait_ge(x_ready, 4 + 3)
            for j in range(U_G):
                if j % 2 == 0:
                    pe.wait_ge(turn_lo, B_XAN + j // 2 + 1)
                u = U_XQ + j
                unit(u, u % SLOTS, xT_hi, 2 * j, xT_lo, 2 * j, pair[0], NW, j == 0, j == U_G - 1)
                if j == 3:
                    pe.wait_ge(x_ready, 8)
                    batch(B_XAN + 3, 0, x_tiles(3))
            pe.wait_ge(qx_ready, 1)
            for h in range(X_HEADS):
                for t in range(NT):
                    tr = nc.tensor.transpose(turn[0][:, h, t * P:(t + 1) * P], qx[:, t, h * X_DH:(h + 1) * X_DH], ident[:])
            tr.then_inc(qx_turned, 1)
            pe.wait_ge(qx_taken, 1)
            for h in range(X_HEADS):
                for t in range(NT):
                    mm = nc.tensor.matmul(psum[:, 4 + h, t * MEM:(t + 1) * MEM], qxT[:, h, t * P:(t + 1) * P],
                                          kxT[:, h, :], start=True, stop=True)
                mm.then_inc(xs_done, 1)
            for h in range(X_HEADS):
                pe.wait_ge(xp_ready, h + 1)
                for k in range(MEM // P):
                    for t in range(NT):
                        tr = nc.tensor.transpose(psum[:, 4 + h, k * SEQ + t * P:k * SEQ + (t + 1) * P],
                                                 px[:, h, t, k * P:(k + 1) * P], ident[:])
                tr.then_inc(xp_turned, 1)
            for h in range(X_HEADS):
                if h == 0:
                    pe.wait_ge(xpT_ready, 2)
                else:
                    pe.wait_ge(xpT_ready, h + 1)
                for k in range(MEM // P):
                    mm = nc.tensor.matmul(turn[0][:, h, :], vx[:, k, h * X_DH:(h + 1) * X_DH], pxT[:, h, k, :],
                                          start=(k == 0), stop=(k == 1))
            mm.then_inc(xo_done, 1)
            pe.wait_ge(xo_lo, 1)
            for n in range(D_CHUNKS):
                if n == 0:
                    pe.wait_ge(x_ready, 8)
                elif n == 1:
                    pe.wait_ge(qx_ready, 1)
                else:
                    pe.wait_ge(x_ready, 8 + n - 1)
                for j in range(U_XOG):
                    u = U_XO + U_XOG * n + j
                    unit(u, u % SLOTS, ffT_hi, OX + 2 * j, ffT_lo, OX + 2 * j, pair[(n + 1) % 2], NW,
                         j == 0, j == U_XOG - 1)
                if n:
                    pe.wait_ge(x_ready, 8 + n)
                    batch(B_F2N + n - 1, 0, x_tiles(n - 1), n > 1)

            ffn_up(U_GU2, B_F2N, B_H2, B_F2N + 3, (x_ready, 12), (x_ready, 11), FF_CHUNKS)
            ffn_down(U_DN2, B_H2, None, FF_CHUNKS, 12)


def constants():
    import numpy as np
    tok = np.arange(P)
    end = np.arange(N_CMP) * CMP_STRIDE + CMP_LEN - 1
    valid = end[None, None, :] <= (tok[:, None, None] + P * np.arange(NT)[None, :, None])
    key = np.arange(SEQ)
    causal = np.where(key[None, :] <= tok[:, None] + P, 0.0, NEG)
    masks = np.zeros((P, len(LEVELS), P // 2), np.float32)
    for l, m in enumerate(LEVELS):
        late = (np.arange(P // (2 * m))[:, None] * 2 * m + m + np.arange(m)[None, :]).ravel()
        hit = (tok[:, None] // (2 * m) == late[None, :] // (2 * m)) & (tok[:, None] % (2 * m) < m)
        masks[:, l, :] = hit
    blk = (tok[:, None] // N_CMP == np.arange(REP)[None, :]).astype(np.float32)
    half = DH // 2
    inv = 10000.0 ** (-np.arange(half, dtype=np.float64) / half)
    return {
        "ident": np.eye(P, dtype=np.float32),
        "inv_f": np.broadcast_to(inv.astype(np.float32), (P, half)).copy(),
        "causal": causal.astype(np.float32),
        "cmp_add": np.where(valid, 0.0, NEG).astype(np.float32),
        "cmp_mul": valid.astype(np.float32),
        "diag_blk": blk,
        "lvl_mask": masks,
    }


def kernel(**inputs):
    import numpy as np
    import concourse.bacc as bacc
    from concourse.bass_utils import run_bass_kernel_spmd

    nc = bacc.Bacc("TRN2", target_bir_lowering=False, num_devices=1)
    laid = {
        "x": inputs["x"][0], "mem": inputs["mem"][0], "pos": inputs["positions"][0],
        "n1": inputs["ffn1_norm"][0], "g1": inputs["ffn1_w_gate"][0], "u1": inputs["ffn1_w_up"][0],
        "d1": inputs["ffn1_w_down"][0], "nm": inputs["mix_norm"][0], "w_in": inputs["w_in"][0],
        "lb": inputs["hgrn_lb_logits"].reshape(-1), "nhg": inputs["hgrn_out_norm"][0],
        "pe": inputs["nsa_cmp_pe"][0].reshape(-1),
        "cw1": np.concatenate([inputs["nsa_cmp_k_w1"][0], inputs["nsa_cmp_v_w1"][0]], axis=1),
        "kw2": inputs["nsa_cmp_k_w2"][0], "vw2": inputs["nsa_cmp_v_w2"][0],
        "w_out": inputs["w_out"][0], "nx": inputs["xattn_norm"][0], "nmem": inputs["mem_norm"][0],
        "wq": inputs["xattn_wq"][0], "wk": inputs["xattn_wk"][0], "wv": inputs["xattn_wv"][0],
        "wo": inputs["xattn_wo"][0], "n2": inputs["ffn2_norm"][0], "g2": inputs["ffn2_w_gate"][0],
        "u2": inputs["ffn2_w_up"][0], "d2": inputs["ffn2_w_down"][0], "fn": inputs["final_norm"],
    }
    arrays, given, tables = {}, {}, {}
    for name, value in laid.items():
        arrays["in_" + name] = np.ascontiguousarray(value)
        given[name] = nc.dram_tensor("in_" + name, arrays["in_" + name].shape,
                                     mybir.dt.from_np(arrays["in_" + name].dtype), kind="ExternalInput").ap()
    for name, value in constants().items():
        arrays["c_" + name] = value
        tables[name] = nc.dram_tensor("c_" + name, value.shape, mybir.dt.from_np(value.dtype),
                                      kind="ExternalInput").ap()
    out = nc.dram_tensor("out", (SEQ, D), F32, kind="ExternalOutput").ap()
    layer_program(nc, given, tables, out)
    r = run_bass_kernel_spmd(nc, [arrays], core_ids=[0])
    return r.results[0]["out"].reshape(1, SEQ, D)
```
